# Optimizing a Trainium2 kernel written in Bass

```python
import math
import jax
import jax.numpy as jnp
from jax import lax
import numpy as np

D_MODEL = 2048
BATCH = 1
SEQ = 512
DEPTH = 1

RMS_EPS = 1e-6
S5_WIDTH = D_MODEL // 2
S5_GROUP = 16
S5_GROUPS = S5_WIDTH // S5_GROUP
S5_STATE = 64
GDN_HEAD_DIM = 128
GDN_WIDTH = D_MODEL // 2
GDN_HEADS = GDN_WIDTH // GDN_HEAD_DIM
CONV_K = 4
CHUNK = 64
N_EXPERTS = 16
N_GROUPS = 4
EXPERTS_PER_GROUP = N_EXPERTS // N_GROUPS
TOP_K = 2
D_FF = D_MODEL // 2
IN_SPLITS = (S5_WIDTH, GDN_WIDTH, GDN_WIDTH, GDN_WIDTH, GDN_WIDTH, GDN_HEADS, GDN_HEADS, D_MODEL, D_MODEL)
IN_COLS = S5_WIDTH + 4 * GDN_WIDTH + 2 * GDN_HEADS + 2 * D_MODEL

kernel_name = "hybrid_s5_gdn_grouped_moe_adaln"

def rmsnorm(x, w):
    xf = x.astype(jnp.float32)
    y = xf * lax.rsqrt(jnp.mean(xf * xf, axis=-1, keepdims=True) + RMS_EPS)
    return (y * w.astype(jnp.float32)).astype(x.dtype)

def l2norm(x):
    return x * lax.rsqrt(jnp.sum(x * x, axis=-1, keepdims=True) + RMS_EPS)

def s5_mixer(u, a_re, a_im, log_dt, b_re, b_im, c_re, c_im, d_skip, w_glu, b_glu):
    bsz, seq, _ = u.shape
    f32 = jnp.float32
    uf = u.astype(f32)
    ug = uf.reshape(bsz, seq, S5_GROUPS, S5_GROUP)
    lam = lax.complex(a_re.astype(f32), a_im.astype(f32))
    dt = jnp.exp(log_dt.astype(f32))[:, None]
    a_bar = jnp.exp(lam * dt)
    b_bar = ((a_bar - 1.0) / lam)[..., None] * lax.complex(b_re.astype(f32), b_im.astype(f32))
    bu = lax.complex(jnp.einsum('blgn,gpn->blgp', ug, b_bar.real),
                     jnp.einsum('blgn,gpn->blgp', ug, b_bar.imag))
    a_seq = jnp.broadcast_to(a_bar, bu.shape)

    def combine(left, right):
        a_l, s_l = left
        a_r, s_r = right
        return a_r * a_l, a_r * s_l + s_r

    _, states = lax.associative_scan(combine, (a_seq, bu), axis=1)
    c_mat = lax.complex(c_re.astype(f32), c_im.astype(f32))
    y = jnp.real(jnp.einsum('blgp,gnp->blgn', states, c_mat)).reshape(bsz, seq, S5_WIDTH)
    y = jax.nn.gelu(y + d_skip.astype(f32) * uf)
    y = y * jax.nn.sigmoid(y @ w_glu.astype(f32) + b_glu.astype(f32))
    return y.astype(u.dtype)

def causal_conv(x, w):
    ch = x.shape[-1]
    return lax.conv_general_dilated(x, w[:, None, :].astype(x.dtype), window_strides=(1,),
                                    padding=[(CONV_K - 1, 0)],
                                    dimension_numbers=('NWC', 'WIO', 'NWC'),
                                    feature_group_count=ch)

def gated_delta_chunked(q, k, v, g, beta):
    bsz, seq, heads, dk = q.shape
    dv = v.shape[-1]
    n_chunks = seq // CHUNK

    def to_chunks(t):
        t = jnp.swapaxes(t, 1, 2)
        return t.reshape(bsz, heads, n_chunks, CHUNK, *t.shape[3:])

    q, k, v, g, beta = (to_chunks(t) for t in (q, k, v, g, beta))
    g = jnp.cumsum(g, axis=-1)
    causal = jnp.tril(jnp.ones((CHUNK, CHUNK), dtype=bool))
    strict = jnp.tril(jnp.ones((CHUNK, CHUNK), dtype=bool), k=-1)
    decay = jnp.exp(jnp.where(causal, g[..., :, None] - g[..., None, :], -jnp.inf))
    k_beta = k * beta[..., None]
    v_beta = v * beta[..., None]
    lmat = jnp.where(strict, jnp.einsum('bhncd,bhnsd->bhncs', k_beta, k) * decay, 0.0)
    eye = jnp.eye(CHUNK, dtype=q.dtype)
    t_inv = lax.linalg.triangular_solve(eye + lmat, jnp.broadcast_to(eye, lmat.shape),
                                        left_side=True, lower=True)
    u = jnp.einsum('bhncs,bhnse->bhnce', t_inv, v_beta)
    w = jnp.einsum('bhncs,bhnsd->bhncd', t_inv, k_beta * jnp.exp(g)[..., None])
    attn = jnp.where(causal, jnp.einsum('bhncd,bhnsd->bhncs', q, k) * decay, 0.0)
    q_dec = q * jnp.exp(g)[..., None]
    g_last = g[..., -1]
    k_dec = k * jnp.exp(g_last[..., None] - g)[..., None]
    xs = tuple(jnp.moveaxis(t, 2, 0) for t in (q_dec, k_dec, u, w, attn, g_last))

    def step(state, inp):
        qd, kd, ui, wi, ai, gl = inp
        v_new = ui - jnp.einsum('bhcd,bhde->bhce', wi, state)
        o = jnp.einsum('bhcd,bhde->bhce', qd, state) + jnp.einsum('bhcs,bhse->bhce', ai, v_new)
        state = state * jnp.exp(gl)[..., None, None] + jnp.einsum('bhcd,bhce->bhde', kd, v_new)
        return state, o

    s0 = jnp.zeros((bsz, heads, dk, dv), q.dtype)
    _, o = lax.scan(step, s0, xs)
    o = jnp.moveaxis(o, 0, 2).reshape(bsz, heads, seq, dv)
    return jnp.swapaxes(o, 1, 2)

def gdn_mixer(q, k, v, z, b_raw, a_raw, conv_w, a_log, dt_bias, out_norm_w):
    bsz, seq, _ = q.shape
    f32 = jnp.float32
    qkv = jax.nn.silu(causal_conv(jnp.concatenate([q, k, v], axis=-1), conv_w)).astype(f32)
    q, k, v = jnp.split(qkv, 3, axis=-1)
    shp = (bsz, seq, GDN_HEADS, GDN_HEAD_DIM)
    q = l2norm(q.reshape(shp)) * (GDN_HEAD_DIM ** -0.5)
    k = l2norm(k.reshape(shp))
    v = v.reshape(shp)
    beta = jax.nn.sigmoid(b_raw.astype(f32))
    g = -jnp.exp(a_log.astype(f32)) * jax.nn.softplus(a_raw.astype(f32) + dt_bias.astype(f32))
    o = gated_delta_chunked(q, k, v, g, beta)
    o = rmsnorm(o, out_norm_w) * jax.nn.silu(z.astype(f32).reshape(shp))
    return o.reshape(bsz, seq, GDN_WIDTH).astype(z.dtype)

def moe(h, w_router, router_bias, w_gate, w_up, w_down):
    bsz, seq, d = h.shape
    x = h.reshape(-1, d)
    f32 = jnp.float32
    scores = jax.nn.sigmoid(x.astype(f32) @ w_router.astype(f32))
    sel = (scores + router_bias.astype(f32)).reshape(-1, N_GROUPS, EXPERTS_PER_GROUP)
    group_score = jnp.sum(lax.top_k(sel, 2)[0], axis=-1)
    best_group = jnp.argmax(group_score, axis=-1)
    in_group = jnp.take_along_axis(sel, best_group[:, None, None], axis=1)[:, 0]
    _, local_idx = lax.top_k(in_group, TOP_K)
    expert_idx = best_group[:, None] * EXPERTS_PER_GROUP + local_idx
    gate_w = jnp.take_along_axis(scores, expert_idx, axis=-1)
    gate_w = gate_w / jnp.sum(gate_w, axis=-1, keepdims=True)
    flat_e = expert_idx.reshape(-1)
    order = jnp.argsort(flat_e)
    tok = order // TOP_K
    group_sizes = jnp.bincount(flat_e, length=N_EXPERTS).astype(jnp.int32)
    xs = x[tok]
    hid = jax.nn.silu(lax.ragged_dot(xs, w_gate, group_sizes)) * lax.ragged_dot(xs, w_up, group_sizes)
    ys = lax.ragged_dot(hid, w_down, group_sizes) * gate_w.reshape(-1)[order][:, None].astype(x.dtype)
    out = jnp.zeros_like(x).at[tok].add(ys)
    return out.reshape(bsz, seq, d)

def setup_inputs(seed: int = 0) -> dict:
    key = jax.random.key(seed)
    ks = jax.random.split(key, 32)
    f32 = jnp.float32
    L = DEPTH

    def nrm(k, shape, scale):
        return jax.random.normal(k, shape, f32) * scale

    x = nrm(ks[0], (BATCH, SEQ, D_MODEL), 1.0)
    c = nrm(ks[1], (BATCH, D_MODEL), 1.0)
    w_ada = nrm(ks[2], (L, D_MODEL, 6 * D_MODEL), 0.5 * D_MODEL ** -0.5)
    b_ada = nrm(ks[3], (L, 6 * D_MODEL), 0.02)
    norm1_w = 1.0 + nrm(ks[4], (L, D_MODEL), 0.02)
    norm2_w = 1.0 + nrm(ks[5], (L, D_MODEL), 0.02)
    w_in = nrm(ks[6], (L, D_MODEL, IN_COLS), D_MODEL ** -0.5)
    n_idx = jnp.arange(S5_STATE, dtype=f32)
    s5_a_re = -0.5 * jnp.exp(nrm(ks[7], (L, S5_GROUPS, S5_STATE), 0.05))
    s5_a_im = math.pi * n_idx + nrm(ks[8], (L, S5_GROUPS, S5_STATE), 0.01)
    s5_log_dt = jax.random.uniform(ks[9], (L, S5_GROUPS), f32, math.log(1e-3), math.log(1e-1))
    s5_b_re = nrm(ks[10], (L, S5_GROUPS, S5_STATE, S5_GROUP), (2 * S5_GROUP) ** -0.5)
    s5_b_im = nrm(ks[11], (L, S5_GROUPS, S5_STATE, S5_GROUP), (2 * S5_GROUP) ** -0.5)
    s5_c_re = nrm(ks[12], (L, S5_GROUPS, S5_GROUP, S5_STATE), 0.5)
    s5_c_im = nrm(ks[13], (L, S5_GROUPS, S5_GROUP, S5_STATE), 0.5)
    s5_d = nrm(ks[14], (L, S5_WIDTH), 1.0)
    s5_w_glu = nrm(ks[15], (L, S5_WIDTH, S5_WIDTH), S5_WIDTH ** -0.5)
    s5_b_glu = nrm(ks[16], (L, S5_WIDTH), 0.02)
    gdn_conv_w = nrm(ks[17], (L, CONV_K, 3 * GDN_WIDTH), CONV_K ** -0.5)
    gdn_a_log = jnp.log(jax.random.uniform(ks[18], (L, GDN_HEADS), f32, 1.0, 16.0))
    gdn_dt = jnp.exp(jax.random.uniform(ks[19], (L, GDN_HEADS), f32, math.log(1e-3), math.log(1e-1)))
    gdn_dt_bias = gdn_dt + jnp.log(-jnp.expm1(-gdn_dt))
    gdn_norm_w = 1.0 + nrm(ks[20], (L, GDN_HEAD_DIM), 0.02)
    w_proj_a = nrm(ks[21], (L, S5_WIDTH, D_MODEL), S5_WIDTH ** -0.5)
    w_proj_b = nrm(ks[22], (L, GDN_WIDTH, D_MODEL), GDN_WIDTH ** -0.5)
    w_out = nrm(ks[23], (L, D_MODEL, D_MODEL), D_MODEL ** -0.5)
    w_router = nrm(ks[24], (D_MODEL, N_EXPERTS), D_MODEL ** -0.5)
    router_bias = nrm(ks[25], (N_EXPERTS,), 0.01)
    w_gate = nrm(ks[26], (L, N_EXPERTS, D_MODEL, D_FF), D_MODEL ** -0.5)
    w_up = nrm(ks[27], (L, N_EXPERTS, D_MODEL, D_FF), D_MODEL ** -0.5)
    w_down = nrm(ks[28], (L, N_EXPERTS, D_FF, D_MODEL), D_FF ** -0.5)
    final_norm_w = 1.0 + nrm(ks[29], (D_MODEL,), 0.02)
    return {"x": x, "c": c, "w_ada": w_ada, "b_ada": b_ada, "norm1_w": norm1_w, "norm2_w": norm2_w,
            "w_in": w_in, "s5_a_re": s5_a_re, "s5_a_im": s5_a_im, "s5_log_dt": s5_log_dt,
            "s5_b_re": s5_b_re, "s5_b_im": s5_b_im, "s5_c_re": s5_c_re, "s5_c_im": s5_c_im,
            "s5_d": s5_d, "s5_w_glu": s5_w_glu, "s5_b_glu": s5_b_glu, "gdn_conv_w": gdn_conv_w,
            "gdn_a_log": gdn_a_log, "gdn_dt_bias": gdn_dt_bias, "gdn_norm_w": gdn_norm_w,
            "w_proj_a": w_proj_a, "w_proj_b": w_proj_b, "w_out": w_out, "w_router": w_router,
            "router_bias": router_bias, "w_gate": w_gate, "w_up": w_up, "w_down": w_down,
            "final_norm_w": final_norm_w}

def reference(x, c, w_ada, b_ada, norm1_w, norm2_w, w_in, s5_a_re, s5_a_im, s5_log_dt,
              s5_b_re, s5_b_im, s5_c_re, s5_c_im, s5_d, s5_w_glu, s5_b_glu, gdn_conv_w,
              gdn_a_log, gdn_dt_bias, gdn_norm_w, w_proj_a, w_proj_b, w_out, w_router,
              router_bias, w_gate, w_up, w_down, final_norm_w):
    split_at = [int(i) for i in np.cumsum(IN_SPLITS)[:-1]]
    c_act = jax.nn.silu(c)
    for l in range(DEPTH):
        mod = (c_act @ w_ada[l] + b_ada[l])[:, None, :]
        sh1, sc1, g1, sh2, sc2, g2 = jnp.split(mod, 6, axis=-1)
        h = rmsnorm(x, norm1_w[l]) * (1.0 + sc1) + sh1
        proj = h @ w_in[l]
        u_s5, q, k, v, z, b_raw, a_raw, gate_a, gate_b = jnp.split(proj, split_at, axis=-1)
        y_a = s5_mixer(u_s5, s5_a_re[l], s5_a_im[l], s5_log_dt[l], s5_b_re[l], s5_b_im[l],
                       s5_c_re[l], s5_c_im[l], s5_d[l], s5_w_glu[l], s5_b_glu[l])
        y_b = gdn_mixer(q, k, v, z, b_raw, a_raw, gdn_conv_w[l], gdn_a_log[l], gdn_dt_bias[l],
                        gdn_norm_w[l])
        merged = (jax.nn.sigmoid(gate_a) * (y_a @ w_proj_a[l])
                  + jax.nn.sigmoid(gate_b) * (y_b @ w_proj_b[l]))
        x = x + g1 * (merged @ w_out[l])
        h2 = rmsnorm(x, norm2_w[l]) * (1.0 + sc2) + sh2
        x = x + g2 * moe(h2, w_router, router_bias, w_gate[l], w_up[l], w_down[l])
    return rmsnorm(x, final_norm_w)


_drawn_inputs = setup_inputs


def setup_inputs(seed=0):
    import zlib

    import numpy as np

    out = dict(_drawn_inputs(seed))
    spreads = {}
    factors = {'norm1_w': 4.569,
     's5_a_re': 200.0,
     's5_b_glu': 64.0,
     'gdn_norm_w': 22.064,
     'final_norm_w': 22.544,
     'norm2_w': 8.0,
     's5_a_im': 3.883,
     's5_log_dt': 4.164,
     's5_b_re': 5.353,
     's5_b_im': 42.136,
     's5_c_re': 5.368,
     's5_c_im': 42.824,
     'router_bias': 5.509}
    for name, (base, spread) in spreads.items():
        noise = np.random.default_rng([zlib.crc32(name.encode()), seed]).standard_normal(out[name].shape)
        drawn = base * np.exp(spread * noise) if base else spread * noise
        out[name] = jnp.asarray(drawn.astype(out[name].dtype))
    for name, factor in factors.items():
        out[name] = (out[name] * factor).astype(out[name].dtype)
    return out
```

```python
from contextlib import ExitStack

import concourse.bass as bass
from concourse import mybir
import numpy as np

F32 = mybir.dt.float32
F32R = mybir.dt.float32r
I32 = mybir.dt.int32
U32 = mybir.dt.uint32
ALU = mybir.AluOpType
ACT = mybir.ActivationFunctionType
AX = mybir.AxisListType

P = 128
D = 2048
T = 512
KD = D // P
EPS = 1e-6
HEADS = 8
CH = 128
NC_ = T // CH
WCOLS = 2048
RING = 3
TILES = 9
SLICES = ((0, 4), (4, 7), (7, 10), (10, 13), (13, 16))
LEVELS = 7
NEG = -1.0e30
EXPERTS = 16
GROUPS = 4
NT = T // P
ITEMS = 24
ECH = 24


def sems(ctx, nc, prefix, names, program=None, pool_dma=""):
    named = {n: ctx.enter_context(nc.semaphore(f"{prefix}_{n}")) for n in names.split()}
    numbers = sorted(x.num for x in named.values())
    starts = [n for n in numbers if n - 1 not in numbers]
    stops = [n + 1 for n in numbers if n + 1 not in numbers]
    for start, stop in zip(starts, stops):
        ctx.callback(nc.all_engine_barrier, sems_to_clear=range(start, stop))
    for n in pool_dma.split():
        named[n] = program.enter_context(nc.semaphore(f"{prefix}_{n}"))
    return named


def split3(pe, out, w_hi, w_lo, a_hi, a_lo, start, stop):
    pe.matmul(out, w_hi, a_hi, start=start, stop=False)
    pe.matmul(out, w_hi, a_lo, start=False, stop=False)
    return pe.matmul(out, w_lo, a_hi, start=False, stop=stop)


def adaln_and_first_norm(nc, d, h_hi, h_lo):
    with ExitStack() as ctx:
        def sb(name, shape, dt=F32):
            return ctx.enter_context(nc.sbuf_tensor("a_" + name, shape, dt))

        s = sems(ctx, nc, "a", "c_in w0 w1 silu c_ready acc_done cols cols_ready ones_set sq_done root rinv xn hf hi lo "
                 "sq_free c_t",
                 d["program"], "x_in small_in c_out")
        landed = (s["w0"], s["w1"])
        x = sb("x", [P, KD, T])
        w_ring = sb("w", [P, 2, WCOLS])
        acc = sb("acc", [P, 2, WCOLS])
        c_raw = sb("c_raw", [P, KD])
        c_tanh = sb("c_tanh", [P, KD])
        c_act = sb("c_act", [P, KD])
        bias = sb("bias", [P, 3, KD])
        mod = sb("mod", [P, 2, KD])
        ones = sb("ones", [P, P])
        eps = sb("eps", [P, 1])
        sq = sb("sq", [P, 2, T])
        root = sb("root", [P, T])
        rinv = sb("rinv", [P, T])
        hf = sb("hf", [P, 2, T])
        ss_ps = ctx.enter_context(nc.psum_tensor("a_ss", [P, T], F32))
        col_ps = ctx.enter_context(nc.psum_tensor("a_col", [P, T], F32))
        block = ctx.enter_context(nc.Block())

        @block.sync
        def _(sp):
            sp.dma_start(c_raw[:], d["c"]).then_inc(s["c_in"], 16)
            for i in range(2 * KD):
                part, kt = i // KD, i % KD
                if i >= 2:
                    sp.wait_ge(s["acc_done"], i - 1)
                sp.dma_start(w_ring[:, i % 2, :],
                             d["w_ada"][kt * P:(kt + 1) * P, part * D:(part + 1) * D]).then_inc(landed[i % 2], 16)

        @block.gpsimd
        def _(pool):
            pool.dma_start(x[:], d["xT"]).then_inc(s["x_in"], 16)
            pool.dma_start(bias[:], d["ada_cols"]).then_inc(s["small_in"], 16)
            pool.wait_ge(s["c_ready"], 1)
            pool.dma_start(d["c_act"], c_act[:]).then_inc(s["c_out"], 16)
            pool.wait_ge(s["c_out"], 16)

        @block.scalar
        def _(act):
            act.wait_ge(s["c_in"], 16)
            act.activation(c_tanh[:], c_raw[:], ACT.Tanh, scale=0.5).then_inc(s["silu"], 1)
            act.wait_ge(s["x_in"], 16)
            for kt in range(KD):
                if kt >= 2:
                    act.wait_ge(s["sq_free"], kt - 1)
                act.activation(sq[:, kt % 2, :], x[:, kt, :], ACT.Square).then_inc(s["sq_done"], 1)
            act.wait_ge(s["sq_free"], KD)
            act.wait_ge(s["ones_set"], 2)
            act.activation(root[:], ss_ps[:], ACT.Sqrt, bias=eps[:, 0:1], scale=1.0 / D).then_inc(s["root"], 1)
            act.wait_ge(s["cols_ready"], 3)
            act.wait_ge(s["xn"], KD)
            for kt in range(KD):
                act.activation(h_hi[:, kt, :], x[:, kt, :], ACT.Identity,
                               bias=mod[:, 0, kt:kt + 1], scale=mod[:, 1, kt:kt + 1]).then_inc(s["hi"], 1)

        @block.vector
        def _(dve):
            dve.memset(ones[:], 1.0).then_inc(s["ones_set"], 1)
            dve.memset(eps[:], EPS).then_inc(s["ones_set"], 1)
            dve.wait_ge(s["silu"], 1)
            dve.scalar_tensor_tensor(c_act[:], c_tanh[:], 1.0, c_raw[:], ALU.add, ALU.mult).then_inc(s["c_t"], 1)
            dve.wait_ge(s["c_t"], 1)
            dve.tensor_scalar(c_act[:], c_act[:], 0.5, None, ALU.mult).then_inc(s["c_ready"], 1)
            dve.wait_ge(s["c_ready"], 1)
            for i in range(2 * KD):
                part, kt = i // KD, i % KD
                dve.wait_ge(landed[i % 2], 16 * (i // 2 + 1))
                if kt == 0:
                    ins = dve.tensor_scalar(acc[:, part, :], w_ring[:, i % 2, :], c_act[:, 0:1], None, ALU.mult)
                else:
                    dve.wait_ge(s["acc_done"], i)
                    ins = dve.scalar_tensor_tensor(acc[:, part, :], w_ring[:, i % 2, :], c_act[:, kt:kt + 1],
                                                   acc[:, part, :], ALU.mult, ALU.add)
                ins.then_inc(s["acc_done"], 1)
                if i == KD - 1:
                    dve.wait_ge(s["root"], 1)
                    dve.reciprocal(rinv[:], root[:]).then_inc(s["rinv"], 1)
                if KD <= i:
                    dve.wait_ge(s["rinv"], 1)
                    dve.tensor_tensor(x[:, i - KD, :], x[:, i - KD, :], rinv[:], ALU.mult).then_inc(s["xn"], 1)
            dve.wait_ge(s["cols"], 1)
            dve.wait_ge(s["small_in"], 16)
            dve.tensor_tensor(mod[:], col_ps[:, 0:2 * KD].rearrange("p (a k) -> p a k", a=2), bias[:, 0:2, :],
                              ALU.add).then_inc(s["cols_ready"], 1)
            dve.wait_ge(s["cols_ready"], 1)
            dve.scalar_tensor_tensor(mod[:, 1, :], mod[:, 1, :], 1.0, bias[:, 2, :], ALU.add,
                                     ALU.mult).then_inc(s["cols_ready"], 1)
            dve.wait_ge(s["cols_ready"], 2)
            dve.sem_inc(s["cols_ready"], 1)
            for kt in range(KD):
                if kt >= 2:
                    dve.wait_ge(s["lo"], kt - 1)
                dve.tensor_scalar(hf[:, kt % 2, :], x[:, kt, :], mod[:, 1, kt:kt + 1], mod[:, 0, kt:kt + 1], ALU.mult,
                                  ALU.add).then_inc(s["hf"], 1)
                dve.wait_ge(s["hf"], kt + 1)
                dve.wait_ge(s["hi"], kt + 1)
                dve.tensor_tensor(h_lo[:, kt, :], hf[:, kt % 2, :], h_hi[:, kt, :].bitcast(F32),
                                  ALU.subtract).then_inc(s["lo"], 1)

        @block.tensor
        def _(pe):
            pe.wait_ge(s["ones_set"], 2)
            for kt in range(KD):
                pe.wait_ge(s["sq_done"], kt + 1)
                mm = pe.matmul(ss_ps[:], ones[:], sq[:, kt % 2, :], start=(kt == 0), stop=(kt == KD - 1))
                mm.then_inc(s["sq_free"], 1)
            pe.wait_ge(s["acc_done"], 2 * KD)
            for part in range(2):
                for kt in range(KD):
                    mm = pe.matmul(col_ps[:, part * KD + kt:part * KD + kt + 1],
                                   acc[:, part, kt * P:(kt + 1) * P], ones[:, 0:1], start=True, stop=True)
            mm.then_inc(s["cols"], 1)


def projections_and_gdn(nc, d, h_hi, h_lo):
    with ExitStack() as ctx:
        def sb(name, shape, dt=F32):
            return ctx.enter_context(nc.sbuf_tensor("g_" + name, shape, dt))

        s = sems(ctx, nc, "g", "raw0 raw1 raw2 hi lo proj evac a_row beta_t beta ax el ln sp_m sp_g g_scan cols_ps cols "
                 "gcopy bcopy neg_h half_h ada_in ada_acc k_cv k_t k2 k_sq q_cv q_t q2 q_sq v_cv v_t v2 "
                 "z_t z2 ss1 root1 rcol bcast kn qn eg glb gdiff edcol gm dt dtb p3 lt lm1 xt0 xt_tr x0 "
                 "attn kd vb kbg_t kbg qd ltm p_ps p_sb x_ps xt_new x_new r1 r vn_ps vn o_ps st_ps state0 "
                 "state o_sb o_sq ss2 root2 rcol2 ro_ps y_w y_n y_out cv init",
                 d["program"], "masks_in consts u_out ada_out gate_out0 gate_out1")
        landed = (s["raw0"], s["raw1"], s["raw2"])
        gate_out = (s["gate_out0"], s["gate_out1"])

        w_raw = sb("w_raw", [P, RING, WCOLS])
        w_hi = sb("w_hi", [P, RING, KD, P], F32R)
        w_lo = sb("w_lo", [P, RING, KD, P], F32R)
        ada_w = sb("ada_w", [P, D])
        ada_acc = sb("ada_acc", [P, D])
        c_act = sb("c_act", [P, 4 * KD])
        conv_w = sb("conv_w", [P, HEADS * 3 * 4])
        norm_w = sb("norm_w", [P, 1])
        dt_bias = sb("dt_bias", [40, 2])
        masks = sb("masks", [P, LEVELS, CH])
        causal = sb("causal", [P, CH])
        ident = sb("ident", [P, P])
        ones_col = sb("ones_col", [P, 1])
        eps_k = sb("eps_k", [P, 3])
        g_col = sb("g_col", [P, HEADS, NC_])
        b_col = sb("b_col", [P, HEADS, NC_])

        kqv_raw = sb("kqv_raw", [P, 3, T + 3])
        kqv = sb("kqv", [P, 3, T])
        z_raw = sb("z_raw", [P, T])
        z2 = sb("z2", [P, T])
        u_sb = sb("u_sb", [P, T])
        gates = sb("gates", [P, 2, T])
        x_sb = sb("x_sb", [P, T])
        xt_sb = sb("xt_sb", [P, T])
        p_sb = sb("p_sb", [P, T])
        eg = sb("eg", [P, T])
        dt_sb = sb("dt_sb", [P, T])
        ltb = sb("ltb", [P, T])
        ltm = sb("ltm", [P, 2, T])
        kd_tok = sb("kd_tok", [P, T])
        vb_tok = sb("vb_tok", [P, T])
        o_sb = sb("o_sb", [P, T])
        o_sq = sb("o_sq", [P, T])
        y_sb = sb("y_sb", [P, T])
        state = sb("state", [P, P])
        rows = (p_sb, eg, kd_tok, vb_tok)
        r_sb = sb("r_sb", [P, P])
        vn_sb = sb("vn_sb", [P, P])
        cols = sb("cols", [P, 12, NC_])
        GH, BH, NGH, HBH, ROOTK, ROOTQ, RK, RQ, GLB, ED, ROOTO, RO = range(12)

        proj_ps = [ctx.enter_context(nc.psum_tensor(f"g_proj{i}", [P, T], F32)) for i in range(RING)]
        a, b, c, e, f = [ctx.enter_context(nc.psum_tensor(f"g_ps{i}", [P, T], F32)) for i in range(5)]
        block = ctx.enter_context(nc.Block())

        K, Q, V = range(3)
        GCHUNK = D // 2
        chunks = lambda t: t.rearrange("p (c n) -> p c n", c=NC_)

        def col(i, c0=0, c1=NC_):
            return cols[:, i, c0:c1]

        @block.sync
        def _(sp):
            def load(slot, index):
                return sp.dma_start(w_raw[:, slot, :], d["w_in"][index].rearrange("a p n -> p (a n)")
                                    ).then_inc(landed[slot], 16)

            load(2, slice(0, 1))
            load(0, slice(1, 2))
            load(1, slice(2, 3))
            with sp.Fori(0, HEADS) as h:
                for j in range(TILES):
                    sp.wait_ge(s["lo"], h * TILES + (j + 1))
                    load((j + 2) % RING, bass.ds(h * TILES + (j + 3), 1))
                    if j < 8:
                        sp.wait_ge(s["ada_acc"], h * 8 + j)
                        sp.dma_start(ada_w[:], d["w_mod"][bass.ds(h * 8 + j, 1)].rearrange("a p n -> (a p) n")
                                     ).then_inc(s["ada_in"], 16)
                sp.wait_ge(s["y_n"], h + 1)
                sp.dma_start(d["y_b"][bass.ds(h, 1)].rearrange("a p n -> (a p) n"), y_sb[:]).then_inc(s["y_out"], 16)
            sp.wait_ge(s["y_out"], 16 * HEADS)
            sp.wait_ge(landed[0], 16 * 25)
            sp.wait_ge(landed[1], 16 * 25)

        @block.gpsimd
        def _(pool):
            pool.dma_start(ident[:], d["ident"]).then_inc(s["masks_in"], 16)
            pool.dma_start(causal[:], d["causal"]).then_inc(s["masks_in"], 16)
            pool.dma_start(masks[:], d["masks"]).then_inc(s["masks_in"], 16)
            pool.dma_start(dt_bias[32:40, :], d["gdn_cols"]).then_inc(s["consts"], 16)
            pool.dma_start(conv_w[:], d["conv_w"]).then_inc(s["consts"], 16)
            pool.dma_start(norm_w[:], d["gdn_norm_w"]).then_inc(s["consts"], 16)
            for n in range(4):
                pool.dma_start(c_act[:, n * KD:(n + 1) * KD], d["c_act"]).then_inc(s["consts"], 16)
            pool.wait_ge(s["masks_in"], 48)
            with pool.Fori(0, HEADS) as h:
                for j in range(TILES):
                    if j == 4:
                        pool.wait_ge(s["lt"], h + 1)
                        for lv in range(1, LEVELS):
                            if lv >= 3:
                                pool.wait_ge(s["p_ps"], h * (LEVELS - 1) + (lv - 2))
                            else:
                                pool.wait_ge(s["p_ps"], h * (LEVELS - 1))
                            pool.tensor_tensor(chunks(ltm[:, lv % 2, :]), chunks(ltb[:]),
                                               masks[:, lv:lv + 1, :].to_broadcast([P, NC_, CH]),
                                               ALU.mult).then_inc(s["ltm"], 1)
                    if j == 5:
                        pool.wait_ge(s["evac"], h * TILES + (4 + 4))
                        pool.wait_ge(s["masks_in"], 48)
                        pool.dma_start(d["u"][bass.ds(h, 1)].rearrange("a p n -> (a p) n"), u_sb[:]
                                       ).then_inc(s["u_out"], 16)
                    if j >= 6:
                        pool.wait_ge(s["evac"], h * TILES + (j - 1 + 4))
                        pool.wait_ge(s["masks_in"], 48)
                        pool.dma_start(d["gates"][bass.ds(h * 4 + (j - 6), 1)].rearrange("a p n -> (a p) n"),
                                       gates[:, (j - 6) % 2, :]).then_inc(gate_out[(j - 6) % 2], 16)
                pool.wait_ge(s["ada_acc"], h * 8 + 8)
                pool.wait_ge(s["masks_in"], 48)
                pool.dma_start(d["ada_sums"][bass.ds(h, 1)].rearrange("a p n -> (a p) n"), ada_acc[:]
                               ).then_inc(s["ada_out"], 16)
                pool.wait_ge(s["evac"], h * TILES + (TILES - 1 + 4))
                pool.wait_ge(s["masks_in"], 48)
                pool.dma_start(d["gates"][bass.ds(h * 4 + 3, 1)].rearrange("a p n -> (a p) n"),
                               gates[:, 1, :]).then_inc(gate_out[1], 16)
            pool.wait_ge(s["u_out"], 16 * HEADS)
            pool.wait_ge(s["ada_out"], 16 * HEADS)
            pool.wait_ge(s["gate_out0"], 16 * 2 * HEADS)
            pool.wait_ge(s["gate_out1"], 16 * 2 * HEADS)

        @block.scalar
        def _(act):
            def split_hi(m, slot, loads, half):
                if half == 0:
                    act.wait_ge(landed[slot], loads)
                    act.wait_ge(s["proj"], m)
                w = w_hi[:, slot].rearrange("p k n -> p (k n)")
                n = WCOLS // 2
                ins = act.activation(w[:, half * n:(half + 1) * n], w_raw[:, slot, half * n:(half + 1) * n], ACT.Copy)
                ins.then_inc(s["hi"], 1)

            for half in range(2):
                split_hi(0, 2, 16, half)
            for half in range(2):
                split_hi(1, 0, 16, half)
            act.wait_ge(s["proj"], 3)
            act.activation(rows[0][0:8, :], proj_ps[2][0:8, :], ACT.Tanh, scale=0.5).then_inc(s["beta_t"], 1)
            act.wait_ge(s["consts"], 112)
            act.activation(rows[0][32:40, :], proj_ps[2][32:40, :], ACT.Identity,
                           bias=dt_bias[32:40, 0:1]).then_inc(s["a_row"], 1)
            act.wait_ge(s["a_row"], 1)
            act.sem_inc(s["evac"], 3)
            act.wait_ge(s["ax"], 1)
            act.activation(rows[2][32:40, :], rows[1][32:40, :], ACT.Exp).then_inc(s["el"], 1)
            act.activation(dt_bias[32:40, 1:2], dt_bias[32:40, 1:2], ACT.Exp).then_inc(s["el"], 1)
            act.wait_ge(s["el"], 2)
            act.activation(rows[3][32:40, :], rows[2][32:40, :], ACT.Ln, bias=1.0).then_inc(s["ln"], 1)

            def evac(h, j):
                bank = proj_ps[j % RING][:]
                act.wait_ge(s["proj"], h * TILES + (j + 4))
                if j < 3:
                    act.wait_ge((s["k_cv"], s["q_cv"], s["v_cv"])[j], h)
                    act.activation(kqv_raw[:, j, 3:], bank, ACT.Copy).then_inc(s["evac"], 1)
                elif j == 3:
                    act.wait_ge(s["z2"], h)
                    act.activation(z_raw[:], bank, ACT.Copy).then_inc(s["evac"], 1)
                elif j == 4:
                    act.wait_ge(s["u_out"], h * 16)
                    act.activation(u_sb[:].rearrange("p (i c) -> p i c", i=8),
                                   bank.rearrange("p (c i) -> p i c", i=8), ACT.Copy).then_inc(s["evac"], 1)
                else:
                    n = j - 5
                    act.wait_ge(gate_out[n % 2], h * 32 + (n // 2) * 16)
                    act.activation(gates[:, n % 2, :], bank, ACT.Tanh, scale=0.5).then_inc(s["evac"], 1)

            def conv_tanh(h, j):
                act.wait_ge((s["k_cv"], s["q_cv"], s["v_cv"])[j], h + 1)
                if j == 0:
                    act.wait_ge(s["x_ps"], h * (LEVELS - 1))
                else:
                    act.wait_ge((s["k2"], s["q2"])[j - 1], h + 1)
                act.activation(p_sb[:], kqv[:, j, :], ACT.Tanh, scale=0.5).then_inc((s["k_t"], s["q_t"], s["v_t"])[j], 1)

            def gdn(h, slot):
                if slot == 7:
                    conv_tanh(h, K)
                if slot == 8:
                    act.wait_ge(s["k2"], h + 1)
                    act.wait_ge(s["p_ps"], h * (LEVELS - 1))
                    act.activation(x_sb[:], kqv[:, K, :], ACT.Square).then_inc(s["k_sq"], 1)
                if slot == 11:
                    conv_tanh(h, Q)
                if slot == 12:
                    act.wait_ge(s["q2"], h + 1)
                    act.wait_ge(s["vn_ps"], h * NC_)
                    act.activation(xt_sb[:], kqv[:, Q, :], ACT.Square).then_inc(s["q_sq"], 1)
                if slot == 13:
                    act.wait_ge(s["ss1"], h + 1)
                    act.wait_ge(s["rcol"], h)
                    act.activation(col(ROOTK), a[:, 0:NC_], ACT.Sqrt, bias=eps_k[:, 0:1]).then_inc(s["root1"], 1)
                    act.activation(col(ROOTQ), a[:, NC_:2 * NC_], ACT.Sqrt, bias=eps_k[:, 1:2],
                                   scale=float(CH)).then_inc(s["root1"], 1)
                if slot == 15:
                    act.wait_ge(s["bcast"], h + 1)
                    act.wait_ge(s["state"], h * NC_)
                    act.activation(eg[:], e[:], ACT.Exp).then_inc(s["eg"], 1)
                    act.wait_ge(s["gdiff"], h)
                    act.activation(col(GLB), chunks(e[:])[:, :, CH - 1], ACT.Copy).then_inc(s["glb"], 1)
                if slot == 16:
                    conv_tanh(h, V)
                    act.wait_ge(s["gdiff"], h + 1)
                    act.activation(col(ED), col(ED), ACT.Exp).then_inc(s["edcol"], 1)
                    act.wait_ge(s["gm"], h + 1)
                    for n in range(NC_):
                        ins = act.activation(dt_sb[:, n * CH:(n + 1) * CH], dt_sb[:, n * CH:(n + 1) * CH], ACT.Exp,
                                             bias=cols[:, NGH, n:n + 1])
                    ins.then_inc(s["dt"], 1)
                if slot == 20:
                    act.wait_ge(s["xt_tr"], h + 1)
                    act.activation(x_sb[:], b[:], ACT.Copy).then_inc(s["x0"], 1)
                if slot == 21:
                    act.wait_ge(s["evac"], h * TILES + (3 + 4))
                    act.wait_ge(s["y_n"], h)
                    act.activation(z2[:], z_raw[:], ACT.Tanh, scale=0.5).then_inc(s["z_t"], 1)
                if 21 <= slot < 21 + 2 * (LEVELS - 1) and (slot - 21) % 2 == 0:
                    n = (slot - 21) // 2
                    act.wait_ge(s["p_ps"], h * (LEVELS - 1) + (n + 1))
                    if n == 0:
                        act.wait_ge(s["v2"], h + 1)
                    else:
                        act.wait_ge(s["x_ps"], h * (LEVELS - 1) + n)
                    act.activation(p_sb[:], c[:], ACT.Copy).then_inc(s["p_sb"], 1)
                if slot in (33, 36, 39, 42):
                    n = (slot - 33) // 3
                    act.wait_ge(s["vn_ps"], h * NC_ + (n + 1))
                    act.wait_ge(s["st_ps"], h * NC_ + n)
                    act.activation(vn_sb[:], f[:, 0:P], ACT.Copy).then_inc(s["vn"], 1)
                if slot == 43:
                    act.wait_ge(s["o_ps"], h * NC_ + NC_)
                    act.wait_ge(s["y_w"], h)
                    act.activation(o_sb[:], b[:], ACT.Copy).then_inc(s["o_sb"], 1)
                    act.wait_ge(s["o_sb"], h + 1)
                    act.wait_ge(s["ss2"], h)
                    act.activation(o_sq[:], o_sb[:], ACT.Square).then_inc(s["o_sq"], 1)
                if slot == 44:
                    act.wait_ge(s["ss2"], h + 1)
                    act.wait_ge(s["rcol2"], h)
                    act.activation(col(ROOTO), a[:, 0:NC_], ACT.Sqrt, bias=eps_k[:, 2:3],
                                   scale=1.0 / CH).then_inc(s["root2"], 1)

            act.wait_ge(s["init"], 6)
            with act.Fori(0, HEADS) as h:
                for j in range(TILES):
                    for i in range(5):
                        if i == 0 and j >= 1:
                            evac(h, j - 1)
                        if i in (0, 2):
                            slot = (j + 1) % RING
                            split_hi(h * TILES + (j + 2), slot,
                                     h * 48 + 16 * ((j + 1) // RING + 1 + (slot == 2)), i // 2)
                        gdn(h, 5 * j + i)
                evac(h, TILES - 1)

        @block.vector
        def _(dve):
            def split_lo(m, slot, loads, half):
                n = WCOLS // 2
                dve.wait_ge(s["hi"], m * 2 - 1 + half)
                w = w_lo[:, slot].rearrange("p k n -> p (k n)")
                hi = w_hi[:, slot].rearrange("p k n -> p (k n)").bitcast(F32)
                ins = dve.tensor_tensor(w[:, half * n:(half + 1) * n], w_raw[:, slot, half * n:(half + 1) * n],
                                        hi[:, half * n:(half + 1) * n], ALU.subtract)
                if half == 1:
                    ins.then_inc(s["lo"], 1)

            dve.memset(ones_col[:], 1.0).then_inc(s["init"], 1)
            dve.memset(eps_k[:, 0:1], 4 * EPS).then_inc(s["init"], 1)
            dve.memset(eps_k[:, 1:2], 4 * EPS * CH).then_inc(s["init"], 1)
            dve.memset(eps_k[:, 2:3], EPS).then_inc(s["init"], 1)
            dve.memset(kqv_raw[:, :, 0:3], 0.0).then_inc(s["init"], 1)
            dve.memset(y_sb[:], 1.0).then_inc(s["cv"], 1)
            dve.wait_ge(s["cv"], 1)
            dve.memset(chunks(y_sb[:])[32:40, :, 0:1], 0.0).then_inc(s["init"], 1)
            for m, slot in ((1, 2), (2, 0)):
                for half in range(2):
                    split_lo(m, slot, 16, half)
            dve.wait_ge(s["beta_t"], 1)
            dve.tensor_scalar(rows[1][0:8, :], rows[0][0:8, :], 1.0, 0.5, ALU.add, ALU.mult).then_inc(s["beta"], 1)
            dve.wait_ge(s["a_row"], 1)
            dve.scalar_tensor_tensor(rows[1][32:40, :], rows[0][32:40, :], -1.0, rows[0][32:40, :], ALU.mult,
                                     ALU.min).then_inc(s["ax"], 1)
            dve.wait_ge(s["ax"], 1)
            dve.tensor_scalar(rows[0][32:40, :], rows[0][32:40, :], 0.0, None, ALU.max).then_inc(s["sp_m"], 1)
            dve.wait_ge(s["ln"], 1)
            dve.wait_ge(s["sp_m"], 1)
            dve.tensor_tensor(rows[0][32:40, :], rows[0][32:40, :], rows[3][32:40, :], ALU.add).then_inc(s["sp_m"], 1)
            dve.wait_ge(s["sp_m"], 2)
            dve.tensor_scalar(rows[0][32:40, :], rows[0][32:40, :], dt_bias[32:40, 1:2], -1.0, ALU.mult,
                              ALU.mult).then_inc(s["sp_g"], 1)
            dve.wait_ge(s["sp_g"], 1)
            dve.wait_ge(s["init"], 6)
            dve.tensor_tensor_scan(rows[1][32:40, :], y_sb[32:40, :], rows[0][32:40, :], 0.0, ALU.mult,
                                   ALU.add).then_inc(s["g_scan"], 1)
            dve.wait_ge(s["cols_ps"], 1)
            dve.tensor_copy(g_col[:].rearrange("p h c -> p c h"),
                            a[:, 0:32].rearrange("p (c h) -> p c h", c=NC_)).then_inc(s["cols"], 1)
            dve.tensor_copy(b_col[:].rearrange("p h c -> p c h"),
                            b[:, 0:32].rearrange("p (c h) -> p c h", c=NC_)).then_inc(s["cols"], 1)
            dve.wait_ge(s["consts"], 112)
            dve.tensor_scalar(norm_w[:], norm_w[:], 0.5, None, ALU.mult).then_inc(s["cols"], 1)
            dve.wait_ge(s["cols"], 3)

            def conv(h, j):
                dve.wait_ge(s["evac"], h * TILES + (j + 4))
                if j == K:
                    dve.wait_ge(s["r1"], h * (NC_ - 1))
                if j == Q:
                    dve.wait_ge(s["o_ps"], h * NC_)
                if j == V:
                    dve.wait_ge(s["p3"], h)
                for tap in range(4):
                    wt = conv_w[:, bass.ds(h * 12 + (j * 4 + tap), 1)]
                    src = kqv_raw[:, j, tap:tap + T]
                    if tap == 0:
                        ins = dve.tensor_scalar(kqv[:, j, :], src, wt, None, ALU.mult)
                    else:
                        dve.wait_ge(s["cv"], h * 9 + (j * 3 + tap + 1))
                        ins = dve.scalar_tensor_tensor(kqv[:, j, :], src, wt, kqv[:, j, :], ALU.mult, ALU.add)
                    ins.then_inc(s["cv"] if tap < 3 else (s["k_cv"], s["q_cv"], s["v_cv"])[j], 1)

            def silu2(h, j):
                dve.wait_ge((s["k_t"], s["q_t"], s["v_t"])[j], h + 1)
                dve.wait_ge((s["k_cv"], s["q_cv"], s["v_cv"])[j], h + 1)
                dve.scalar_tensor_tensor(kqv[:, j, :], p_sb[:], 1.0, kqv[:, j, :], ALU.add,
                                         ALU.mult).then_inc((s["k2"], s["q2"], s["v2"])[j], 1)

            def gdn(h, slot):
                if slot == 0:
                    dve.wait_ge(s["bcast"], h)
                    dve.wait_ge(s["dt"], h)
                    dve.wait_ge(s["vb"], h)
                    dve.tensor_copy(col(GH), g_col[:, bass.ds(h, 1), :].rearrange("p a c -> p (a c)")).then_inc(s["gcopy"], 1)
                    dve.tensor_copy(col(BH), b_col[:, bass.ds(h, 1), :].rearrange("p a c -> p (a c)")).then_inc(s["bcopy"], 1)
                    dve.wait_ge(s["gcopy"], h + 1)
                    dve.tensor_scalar(col(NGH), col(GH), -1.0, None, ALU.mult).then_inc(s["neg_h"], 1)
                    dve.wait_ge(s["bcopy"], h + 1)
                    dve.tensor_scalar(col(HBH), col(BH), 0.5, None, ALU.mult).then_inc(s["half_h"], 1)
                    dve.wait_ge(s["st_ps"], h * NC_)
                    dve.wait_ge(s["state"], h * NC_)
                    dve.memset(state[:], 0.0).then_inc(s["state0"], 1)
                if slot == 5:
                    conv(h, K)
                if slot == 8:
                    silu2(h, K)
                if slot == 10:
                    conv(h, Q)
                if slot == 12:
                    silu2(h, Q)
                if slot == 13:
                    dve.wait_ge(s["root1"], 2 * h + 2)
                    dve.reciprocal(cols[:, RK:RQ + 1, :], cols[:, ROOTK:ROOTQ + 1, :]).then_inc(s["rcol"], 1)
                if slot == 15:
                    conv(h, V)
                    dve.wait_ge(s["bcast"], h + 1)
                    dve.tensor_tensor(kqv[:, K, :], kqv[:, K, :], b[:], ALU.mult).then_inc(s["kn"], 1)
                    dve.tensor_tensor(kqv[:, Q, :], kqv[:, Q, :], c[:], ALU.mult).then_inc(s["qn"], 1)
                if slot == 16:
                    dve.wait_ge(s["glb"], h + 1)
                    dve.tensor_tensor(col(ED), col(GLB), col(GH), ALU.subtract).then_inc(s["gdiff"], 1)
                    dve.wait_ge(s["o_ps"], h * NC_)
                    dve.tensor_tensor(chunks(dt_sb[:]), chunks(e[:]),
                                      causal[:].rearrange("p (a n) -> p a n", a=1).to_broadcast([P, NC_, CH]),
                                      ALU.add).then_inc(s["gm"], 1)
                if slot == 17:
                    silu2(h, V)
                    dve.wait_ge(s["dt"], h + 1)
                    dve.wait_ge(s["ltm"], h * (LEVELS - 1))
                    dve.tensor_tensor(ltb[:], dt_sb[:], f[:], ALU.mult).then_inc(s["dtb"], 1)
                    dve.wait_ge(s["eg"], h + 1)
                    dve.wait_ge(s["y_out"], h * 16)
                    dve.tensor_tensor(y_sb[:], eg[:], f[:], ALU.mult).then_inc(s["kbg_t"], 1)
                if slot == 18:
                    dve.wait_ge(s["p3"], h + 1)
                    dve.wait_ge(s["dtb"], h + 1)
                    dve.tensor_tensor(ltb[:], ltb[:], b[:], ALU.mult).then_inc(s["lt"], 1)
                    dve.wait_ge(s["lt"], h + 1)
                    dve.tensor_tensor(chunks(xt_sb[:]), chunks(ltb[:]),
                                      masks[:, 0:1, :].to_broadcast([P, NC_, CH]), ALU.mult).then_inc(s["lm1"], 1)
                    dve.wait_ge(s["lm1"], h + 1)
                    dve.tensor_tensor(chunks(xt_sb[:]),
                                      ident[:].rearrange("p (a n) -> p a n", a=1).to_broadcast([P, NC_, CH]),
                                      chunks(xt_sb[:]), ALU.subtract).then_inc(s["xt0"], 1)
                    dve.tensor_tensor(dt_sb[:], dt_sb[:], c[:], ALU.mult).then_inc(s["attn"], 1)
                if slot == 20:
                    dve.wait_ge(s["edcol"], h + 1)
                    dve.wait_ge(s["st_ps"], h * NC_)
                    dve.wait_ge(s["half_h"], h + 1)
                    dve.tensor_tensor(chunks(kd_tok[:]), chunks(e[:]),
                                      cols[:, ED, :].rearrange("p (c a) -> p c a", a=1).to_broadcast([P, NC_, CH]),
                                      ALU.mult).then_inc(s["kd"], 1)
                    dve.tensor_tensor(chunks(vb_tok[:]), chunks(a[:]),
                                      cols[:, HBH, :].rearrange("p (c a) -> p c a", a=1).to_broadcast([P, NC_, CH]),
                                      ALU.mult).then_inc(s["vb"], 1)
                    dve.tensor_tensor(kqv[:, Q, :], kqv[:, Q, :], eg[:], ALU.mult).then_inc(s["qd"], 1)
                    dve.wait_ge(s["kbg_t"], h + 1)
                    dve.tensor_tensor(kqv[:, K, :], kqv[:, K, :], y_sb[:], ALU.mult).then_inc(s["kbg"], 1)
                if slot == 23:
                    dve.wait_ge(s["z_t"], h + 1)
                    dve.scalar_tensor_tensor(z2[:], z2[:], 1.0, z_raw[:], ALU.add, ALU.mult).then_inc(s["z2"], 1)
                if 22 <= slot <= 32 and slot % 2 == 0:
                    n = (slot - 22) // 2
                    dve.wait_ge(s["x_ps"], h * (LEVELS - 1) + (n + 1))
                    dve.tensor_tensor(xt_sb[:], xt_sb[:], b[:], ALU.subtract).then_inc(s["xt_new"], 1)
                    if n < LEVELS - 2:
                        dve.tensor_tensor(x_sb[:], x_sb[:], e[:], ALU.subtract).then_inc(s["x_new"], 1)
                if slot in (35, 38, 41):
                    n = (slot - 32) // 3
                    blk = vb_tok[:, n * CH:(n + 1) * CH]
                    dve.wait_ge(s["vn_ps"], h * NC_ + n)
                    dve.wait_ge(s["r1"], h * (NC_ - 1) + n)
                    dve.tensor_tensor(r_sb[:], blk, a[:, 0:P], ALU.subtract).then_inc(s["r"], 1)
                if slot in (34, 37, 40, 43):
                    n = (slot - 34) // 3
                    dve.wait_ge(s["st_ps"], h * NC_ + (n + 1))
                    if n == 0:
                        dve.wait_ge(s["state0"], h + 1)
                    else:
                        dve.wait_ge(s["state"], h * NC_ + n)
                    dve.scalar_tensor_tensor(state[:], state[:], eg[:, n * CH + CH - 1:n * CH + CH], e[:, 0:P],
                                             ALU.mult, ALU.add).then_inc(s["state"], 1)
                if slot == 44:
                    dve.wait_ge(s["root2"], h + 1)
                    dve.reciprocal(col(RO), col(ROOTO)).then_inc(s["rcol2"], 1)

            with dve.Fori(0, HEADS) as h:
                for j in range(TILES):
                    for i in range(5):
                        if i in (0, 2):
                            slot = (j + 1) % RING
                            split_lo(h * TILES + (j + 3), slot, None, i // 2)
                        if j < 8 and i in (1, 3):
                            half = i // 2
                            if i == 1:
                                dve.wait_ge(s["ada_in"], h * 128 + 16 * (j + 1))
                                if j == 0:
                                    dve.wait_ge(s["ada_out"], h * 16)
                                else:
                                    dve.wait_ge(s["ada_acc"], h * 8 + j)
                            n = slice(half * GCHUNK, (half + 1) * GCHUNK)
                            ck = c_act[:, bass.ds(h * 8 + j, 1)]
                            if j == 0:
                                ins = dve.tensor_scalar(ada_acc[:, n], ada_w[:, n], ck, None, ALU.mult)
                            else:
                                ins = dve.scalar_tensor_tensor(ada_acc[:, n], ada_w[:, n], ck, ada_acc[:, n],
                                                               ALU.mult, ALU.add)
                            if i == 3:
                                ins.then_inc(s["ada_acc"], 1)
                        gdn(h, 5 * j + i)
                dve.wait_ge(s["ro_ps"], h + 1)
                dve.scalar_tensor_tensor(y_sb[:], o_sb[:], norm_w[:, 0:1], b[:], ALU.mult, ALU.mult).then_inc(s["y_w"], 1)
                dve.wait_ge(s["y_w"], h + 1)
                dve.tensor_tensor(y_sb[:], y_sb[:], z2[:], ALU.mult).then_inc(s["y_n"], 1)

        @block.tensor
        def _(pe):
            def transposes(out, src):
                for n in range(NC_):
                    ins = pe.transpose(out[:, n * CH:(n + 1) * CH], src[:, n * CH:(n + 1) * CH], ident[:])
                return ins

            def products(out, lhs, rhs):
                for n in range(NC_):
                    blk = slice(n * CH, (n + 1) * CH)
                    ins = pe.matmul(out[:, blk], lhs[:, blk], rhs[:, blk], start=True, stop=True)
                return ins

            def over_partitions(out, i):
                for n in range(NC_):
                    ins = pe.matmul(out[:, n * CH:(n + 1) * CH], cols[:, i, n:n + 1].to_broadcast([P, P]), ident[:],
                                    start=True, stop=True)
                return ins

            def project(bank, slot, k0, k1):
                for k in range(k0, k1):
                    ins = split3(pe, bank[:], w_hi[:, slot, k, :], w_lo[:, slot, k, :], h_hi[:, k, :], h_lo[:, k, :],
                                 k == 0, k == KD - 1)
                if k1 == KD:
                    ins.then_inc(s["proj"], 1)

            def gdn(h, slot):
                if slot == 13:
                    pe.wait_ge(s["k_sq"], h + 1)
                    pe.wait_ge(s["q_sq"], h + 1)
                    pe.wait_ge(s["root2"], h)
                    for i, sq in enumerate((x_sb, xt_sb)):
                        for n in range(NC_):
                            ins = pe.matmul(a[:, i * NC_ + n:i * NC_ + n + 1], sq[:, n * CH:(n + 1) * CH], ones_col[:],
                                            start=True, stop=True)
                    ins.then_inc(s["ss1"], 1)
                if slot == 14:
                    pe.wait_ge(s["rcol"], h + 1)
                    pe.wait_ge(s["gcopy"], h + 1)
                    pe.wait_ge(s["bcopy"], h + 1)
                    pe.wait_ge(s["y_w"], h)
                    pe.wait_ge(s["p_sb"], h * (LEVELS - 1))
                    pe.wait_ge(s["state"], h * NC_)
                    pe.wait_ge(s["vn"], h * NC_)
                    over_partitions(b, RK)
                    over_partitions(c, RQ)
                    over_partitions(e, GH)
                    over_partitions(f, BH).then_inc(s["bcast"], 1)
                if slot == 18:
                    pe.wait_ge(s["kn"], h + 1)
                    pe.wait_ge(s["qn"], h + 1)
                    pe.wait_ge(s["glb"], h + 1)
                    pe.wait_ge(s["gm"], h + 1)
                    pe.wait_ge(s["v2"], h + 1)
                    pe.wait_ge(s["root1"], 2 * h + 2)
                    products(b, kqv[:, K, :], kqv[:, K, :])
                    products(c, kqv[:, K, :], kqv[:, Q, :])
                    transposes(e, kqv[:, K, :])
                    transposes(a, kqv[:, V, :]).then_inc(s["p3"], 1)
                if slot == 19:
                    pe.wait_ge(s["xt0"], h + 1)
                    transposes(b, xt_sb[:]).then_inc(s["xt_tr"], 1)
                if 21 <= slot < 21 + 2 * (LEVELS - 1):
                    n = (slot - 21) // 2
                    if (slot - 21) % 2 == 0:
                        pe.wait_ge(s["ltm"], h * (LEVELS - 1) + (n + 1))
                        if n == 0:
                            pe.wait_ge(s["x0"], h + 1)
                            pe.wait_ge(s["attn"], h + 1)
                        else:
                            pe.wait_ge(s["x_new"], h * (LEVELS - 2) + n)
                            pe.wait_ge(s["p_sb"], h * (LEVELS - 1) + n)
                        products(c, ltm[:, (n + 1) % 2, :], x_sb[:]).then_inc(s["p_ps"], 1)
                    else:
                        pe.wait_ge(s["p_sb"], h * (LEVELS - 1) + (n + 1))
                        if n == 0:
                            pe.wait_ge(s["kd"], h + 1)
                        else:
                            pe.wait_ge(s["xt_new"], h * (LEVELS - 1) + n)
                            pe.wait_ge(s["x_new"], h * (LEVELS - 2) + n)
                        ins = products(b, p_sb[:], xt_sb[:])
                        if n < LEVELS - 2:
                            ins = products(e, xt_sb[:], p_sb[:])
                        ins.then_inc(s["x_ps"], 1)
                if slot in (33, 36, 39, 42):
                    n = (slot - 33) // 3
                    pe.wait_ge(s["vb"], h + 1)
                    if n == 0:
                        pe.wait_ge(s["xt_new"], h * (LEVELS - 1) + (LEVELS - 1))
                        pe.wait_ge(s["kbg_t"], h + 1)
                        r = vb_tok[:, 0:CH]
                    else:
                        pe.wait_ge(s["r"], h * (NC_ - 1) + n)
                        pe.wait_ge(s["vn"], h * NC_ + n)
                        r = r_sb[:]
                    pe.matmul(f[:, 0:P], xt_sb[:, n * CH:(n + 1) * CH], r, start=True, stop=True).then_inc(s["vn_ps"], 1)
                if slot in (34, 37, 40, 43):
                    n = (slot - 34) // 3
                    blk = slice(n * CH, (n + 1) * CH)
                    pe.wait_ge(s["vn"], h * NC_ + (n + 1))
                    if n == 0:
                        pe.wait_ge(s["qd"], h + 1)
                    else:
                        pe.wait_ge(s["state"], h * NC_ + n)
                        pe.matmul(b[:, blk], state[:], kqv[:, Q, blk], start=True, stop=False)
                    pe.matmul(b[:, blk], vn_sb[:], dt_sb[:, blk], start=(n == 0), stop=True).then_inc(s["o_ps"], 1)
                    if n == 0:
                        pe.wait_ge(s["x_new"], h * (LEVELS - 2) + (LEVELS - 2))
                    pe.matmul(e[:, 0:P], kd_tok[:, blk], vn_sb[:], start=True, stop=True).then_inc(s["st_ps"], 1)
                if slot in (35, 38, 41):
                    n = (slot - 32) // 3
                    blk = slice(n * CH, (n + 1) * CH)
                    pe.wait_ge(s["state"], h * NC_ + n)
                    pe.wait_ge(s["kbg"], h + 1)
                    if n > 1:
                        pe.wait_ge(s["r"], h * (NC_ - 1) + (n - 1))
                    pe.matmul(a[:, 0:P], kqv[:, K, blk], state[:], start=True, stop=True).then_inc(s["r1"], 1)
                if slot == 44:
                    pe.wait_ge(s["o_sq"], h + 1)
                    pe.wait_ge(s["r"], h * (NC_ - 1) + (NC_ - 1))
                    for n in range(NC_):
                        ins = pe.matmul(a[:, n:n + 1], o_sq[:, n * CH:(n + 1) * CH], ones_col[:], start=True, stop=True)
                    ins.then_inc(s["ss2"], 1)

            pe.sem_inc(s["proj"], 2)
            pe.wait_ge(s["hi"], 2)
            pe.wait_ge(s["lo"], 1)
            project(proj_ps[2], 2, 0, KD)
            pe.wait_ge(s["masks_in"], 48)
            pe.wait_ge(s["beta"], 1)
            pe.wait_ge(s["g_scan"], 1)
            for n in range(NC_):
                pe.transpose(a[:, n * HEADS:(n + 1) * HEADS], rows[1][32:40, n * CH:(n + 1) * CH], ident[32:40, 32:40])
                ins = pe.transpose(b[:, n * HEADS:(n + 1) * HEADS], rows[1][0:8, n * CH:(n + 1) * CH],
                                   ident[0:8, 0:8])
            ins.then_inc(s["cols_ps"], 1)
            pe.wait_ge(s["cols"], 2)
            pe.wait_ge(s["init"], 6)
            with pe.Fori(0, HEADS) as h:
                for j in range(TILES):
                    for i, (k0, k1) in enumerate(SLICES):
                        if i == 0:
                            pe.wait_ge(s["hi"], h * (2 * TILES) + 2 * (j + 2))
                            pe.wait_ge(s["lo"], h * TILES + (j + 2))
                            pe.wait_ge(s["evac"], h * TILES + (j + 1))
                        project(proj_ps[j % RING], j % RING, k0, k1)
                        gdn(h, 5 * j + i)
                pe.wait_ge(s["rcol2"], h + 1)
                pe.wait_ge(s["o_sb"], h + 1)
                over_partitions(b, RO).then_inc(s["ro_ps"], 1)


def s5_branch(nc, d, y_feat):
    G, ST, M, L, NCH = 64, 64, 16, 8, 64
    NT = 17
    OCT = 8
    ROUND = 1.5 * 2.0 ** 23
    TURN = 6.283185
    with ExitStack() as ctx:
        def sb(name, shape, dt=F32):
            return ctx.enter_context(nc.sbuf_tensor("s_" + name, shape, dt))

        s = sems(ctx, nc, "s", "in_par in_b in_c in_u0 in_ident dt x turns px py rnd fr fr2 th half sin cos den rden pw "
                 "ar ai em den2 f1 f2 f3 f4 f5 bx1 bx by1 by cx ncx nc2 cang crnd cfr ccos csin cspm c1a "
                 "c1 c2a c2b c2 ba bp bt_ps bt k_ps kpad kz k_out t_in bxo y_feat v_ps z1 z2 scan w1 y_ps "
                 "y_sb y_out")
        par = sb("par", [P, 3, G])
        consts = sb("consts", [P, NT + NCH + 2])
        b1, b2 = sb("b1", [P, G, M]), sb("b2", [P, G, M])
        c1i, c2i = sb("c1i", [P, G, M]), sb("c2i", [P, G, M])
        bx, by = sb("bx", [P, G, M]), sb("by", [P, G, M])
        cx, ncx, nc2 = sb("cx", [P, G, M]), sb("ncx", [P, G, M]), sb("nc2", [P, G, M])
        small = sb("small", [P, 12, G])
        DT, X, TU, EM, RE, IM, DEN, FR, FI, T1, T2, T3 = range(12)
        ar, ai = sb("ar", [P, G, NT]), sb("ai", [P, G, NT])
        pa, pb, pc, pd = (sb(n, [P, G, NT]) for n in ("pa", "pb", "pc", "pd"))
        cosc, sinc, spm = sb("cosc", [P, G, NCH]), sb("sinc", [P, G, NCH]), sb("spm", [P, G, NCH])
        u_all = sb("u_all", [P, G, NCH])
        quad = lambda t, n: t[:].rearrange("p (g t) n -> p g (t n)", g=n)
        t_sb = (sb("t", [P, OCT, P])[:], quad(b2, OCT))
        c1 = (sb("c1a", [P, OCT, L + 1, M]), sb("c1b", [P, OCT, L + 1, M]))
        c2 = (sb("c2", [P, OCT, L, M])[:], b1[:].rearrange("p (g t) n -> p g t n", g=OCT))
        c2t = sb("c2t", [P, OCT, L, M])
        bp = sb("bp", [P, OCT, L, M])
        tmp = sb("tmp", [P, OCT, L + 1, M])
        bt = sb("bt", [P, OCT, 3 * ST])
        bxo = sb("bxo", [P, OCT, M])
        kpad = sb("kpad", [M, OCT, (2 * L - 1) * M])
        z1 = (sb("z1", [P, OCT, NCH])[:], quad(c1i, 2 * OCT)[:, 0:OCT, :])
        z2 = (sb("z2", [P, OCT, NCH])[:], quad(c1i, 2 * OCT)[:, OCT:2 * OCT, :])
        z = sb("z", [P, OCT, NCH])
        y_sb = sb("y", [P, OCT, NCH])
        ident = sb("ident", [P, P])

        v_ps = ctx.enter_context(nc.psum_tensor("s_v", [P, T], F32))
        vs_ps = ctx.enter_context(nc.psum_tensor("s_vs", [P, T], F32))
        y_ps = ctx.enter_context(nc.psum_tensor("s_yp", [P, T], F32))
        bt_ps = ctx.enter_context(nc.psum_tensor("s_btp", [P, 2 * T], F32))
        k_ps = ctx.enter_context(nc.psum_tensor("s_kp", [P, 2 * T], F32))
        block = ctx.enter_context(nc.Block())

        NK = L + 1
        v = lambda i: small[:, i, :]

        def octets(eng, step):
            with eng.Fori(0, G // OCT // 2 - 1) as pair:
                for par in range(2):
                    step(pair * 2 + par, par)
            step(G // OCT - 2, 0)
            step(G // OCT - 1, 1, last=True)

        @block.sync
        def _(sp):
            sp.dma_start(par[:], d["s5_par"]).then_inc(s["in_par"], 16)
            sp.dma_start(consts[:], d["s5_const"]).then_inc(s["in_par"], 16)
            sp.dma_start(b1[:], d["s5_b"][:, 0]).then_inc(s["in_b"], 16)
            sp.dma_start(b2[:], d["s5_b"][:, 1]).then_inc(s["in_b"], 16)
            sp.dma_start(c1i[:], d["s5_c"][:, 0]).then_inc(s["in_c"], 16)
            sp.dma_start(c2i[:], d["s5_c"][:, 1]).then_inc(s["in_c"], 16)
            sp.dma_start(ident[:], d["ident"]).then_inc(s["in_ident"], 16)
            u_src = d["u"].rearrange("o (g m) (j c) -> j m (o g) c", m=M, j=L)
            for j in range(L):
                sp.dma_start(u_all[j * M:(j + 1) * M, :, :], u_src[j]).then_inc(s["in_u0"], 16)

            def toeplitz(o, par):
                sp.wait_ge(s["kpad"], o + 1)
                sp.dma_start(d["s5_k"][bass.ds(o, 1)].rearrange("a m g n -> (a m) g n"), kpad[:]).then_inc(s["k_out"], 16)
                sp.wait_ge(s["k_out"], o * 16 + 16)
                for j in range(L):
                    sp.dma_start(t_sb[par][j * M:(j + 1) * M, :, :],
                                 d["s5_k"][bass.ds(o, 1), :, :, (L - 1 - j) * M:(L - 1 - j) * M + P]
                                 .rearrange("a m g n -> (a m) g n")).then_inc(s["t_in"], 16)

            def step(o, par, last=False):
                if not last:
                    toeplitz(o + 1, 1 - par)
                sp.wait_ge(s["y_sb"], o + 1)
                sp.dma_start(d["s5_y"][bass.ds(o, 1)].rearrange("a p n -> (a p) n"),
                             y_sb[:].rearrange("p g c -> p (g c)")).then_inc(s["y_out"], 16)
                sp.wait_ge(s["y_out"], o * 16 + 16)
                y_src = d["s5_y"][bass.ds(o, 1)].rearrange("a (i n) (g c) -> (a g) n i c", n=M, g=OCT)
                for g in range(OCT):
                    sp.dma_start(y_feat[g * M:(g + 1) * M, bass.ds(o, 1), :].rearrange("n a (i c) -> n (a i) c", i=L),
                                 y_src[g]).then_inc(s["y_feat"], 16)

            toeplitz(0, 0)
            octets(sp, step)
            sp.wait_ge(s["y_feat"], 16 * G)

        @block.gpsimd
        def _(pool):
            pool.memset(kpad[:], 0.0).then_inc(s["kz"], 1)
            pool.wait_ge(s["cx"], 1)
            pool.wait_ge(s["ncx"], 1)
            pool.wait_ge(s["nc2"], 1)
            pool.wait_ge(s["ai"], 1)
            pool.wait_ge(s["by"], 1)

            def powers(o, par, free=None):
                grp = bass.ds(o * OCT, OCT)
                if free is not None:
                    pool.wait_ge(s["y_ps"], free)
                pool.tensor_tensor(c2[par], ar[:, grp, 1:NK].rearrange("p g (t a) -> p g t a", a=1).to_broadcast([P, OCT, L, M]),
                                   nc2[:, grp, :].rearrange("p g (a n) -> p g a n", a=1).to_broadcast([P, OCT, L, M]),
                                   ALU.mult).then_inc(s["c2a"], 1)
                pool.wait_ge(s["c2"], o)
                pool.tensor_tensor(c2t[:], ai[:, grp, 1:NK].rearrange("p g (t a) -> p g t a", a=1).to_broadcast([P, OCT, L, M]),
                                   ncx[:, grp, :].rearrange("p g (a n) -> p g a n", a=1).to_broadcast([P, OCT, L, M]),
                                   ALU.mult).then_inc(s["c2b"], 1)
                pool.wait_ge(s["c2a"], o + 1)
                pool.wait_ge(s["c2b"], o + 1)
                pool.tensor_tensor(c2[par], c2[par], c2t[:], ALU.add).then_inc(s["c2"], 1)

            def step(o, par, last=False):
                if not last:
                    powers(o + 1, 1 - par, o)

            powers(0, 0)
            octets(pool, step)

        @block.scalar
        def _(act):
            act.wait_ge(s["in_par"], 32)
            act.activation(v(DT), par[:, 2, :], ACT.Exp).then_inc(s["dt"], 1)
            act.wait_ge(s["px"], 1)
            act.activation(pa[:], pa[:], ACT.Tanh, scale=0.5).then_inc(s["th"], 1)
            act.wait_ge(s["fr"], 1)
            act.activation(v(T1), pb[:, :, 1], ACT.Sin, scale=0.5 * TURN).then_inc(s["half"], 1)
            act.activation(ai[:], pb[:], ACT.Sin, scale=TURN).then_inc(s["sin"], 1)
            act.wait_ge(s["fr2"], 1)
            act.activation(ar[:], pc[:], ACT.Sin, scale=TURN).then_inc(s["cos"], 1)
            act.wait_ge(s["cfr"], 1)
            act.activation(sinc[:], sinc[:], ACT.Sin, scale=TURN).then_inc(s["csin"], 1)
            act.wait_ge(s["cfr"], 2)
            act.activation(cosc[:], cosc[:], ACT.Sin, scale=TURN).then_inc(s["ccos"], 1)

            def transposed(o):
                act.wait_ge(s["bt_ps"], o + 1)
                act.wait_ge(s["v_ps"], o)
                src = bt_ps[:].rearrange("p (g n) -> p g n", g=OCT)
                act.activation(bt[:, :, 0:P], src, ACT.Copy).then_inc(s["bt"], 1)
                act.activation(bt[:, :, P:3 * ST], src[:, :, 0:ST], ACT.Copy).then_inc(s["bt"], 1)

            def responses(o):
                act.wait_ge(s["k_ps"], o + 1)
                act.wait_ge(s["k_out"], o * 16)
                act.activation(kpad[:, :, (L - 1) * M:], k_ps[0:M, :].rearrange("p (g n) -> p g n", g=OCT),
                               ACT.Copy).then_inc(s["kpad"], 1)

            def step(o, par, last=False):
                if not last:
                    transposed(o + 1)
                    responses(o + 1)
                act.wait_ge(s["y_ps"], o + 1)
                act.wait_ge(s["y_out"], o * 16)
                act.activation(y_sb[:].rearrange("p g c -> p (g c)"), y_ps[:], ACT.Copy).then_inc(s["y_sb"], 1)

            act.wait_ge(s["kz"], 1)
            transposed(0)
            responses(0)
            octets(act, step)

        @block.vector
        def _(dve):
            def mul(out, x, y, sem, op=ALU.mult):
                return dve.tensor_tensor(out, x, y, op).then_inc(sem, 1)

            gt = lambda x: x.rearrange("p (g a) -> p g a", a=1).to_broadcast([P, G, NT])
            gm = lambda x: x.rearrange("p (g a) -> p g a", a=1).to_broadcast([P, G, M])
            gc = lambda x: x.rearrange("p (g a) -> p g a", a=1).to_broadcast([P, G, NCH])
            powers = consts[:, 0:NT].rearrange("p (a t) -> p a t", a=1).to_broadcast([P, G, NT])
            starts = consts[:, NT:NT + NCH].rearrange("p (a t) -> p a t", a=1).to_broadcast([P, G, NCH])
            sgn = consts[:, NT + NCH:NT + NCH + 1]
            nsgn = consts[:, NT + NCH + 1:NT + NCH + 2]

            dve.wait_ge(s["dt"], 1)
            mul(v(X), par[:, 0, :], v(DT), s["x"])
            mul(v(TU), par[:, 1, :], v(DT), s["turns"])
            dve.wait_ge(s["turns"], 1)
            dve.tensor_scalar(v(TU), v(TU), 1.0 / (2.0 * np.pi), None, ALU.mult).then_inc(s["turns"], 1)
            dve.wait_ge(s["x"], 1)
            mul(pa[:], gt(v(X)), powers, s["px"])
            dve.wait_ge(s["turns"], 2)
            mul(pb[:], gt(v(TU)), powers, s["py"])
            dve.wait_ge(s["py"], 1)
            dve.tensor_scalar(pc[:], pb[:], ROUND, ROUND, ALU.add, ALU.subtract).then_inc(s["rnd"], 1)
            dve.wait_ge(s["rnd"], 1)
            mul(pb[:], pb[:], pc[:], s["fr"], ALU.subtract)
            dve.wait_ge(s["fr"], 1)
            dve.tensor_scalar(pc[:], pb[:], 0.25, None, ALU.add).then_inc(s["rnd"], 1)
            dve.wait_ge(s["rnd"], 2)
            dve.wait_ge(s["th"], 1)
            dve.tensor_scalar(pd[:], pc[:], ROUND, ROUND, ALU.add, ALU.subtract).then_inc(s["rnd"], 1)
            dve.wait_ge(s["rnd"], 3)
            mul(pc[:], pc[:], pd[:], s["fr2"], ALU.subtract)
            dve.wait_ge(s["fr2"], 1)
            dve.wait_ge(s["half"], 1)
            dve.wait_ge(s["sin"], 1)
            dve.tensor_scalar(pb[:], pa[:], -1.0, 1.0, ALU.mult, ALU.add).then_inc(s["den"], 1)
            dve.wait_ge(s["den"], 1)
            dve.reciprocal(pd[:], pb[:]).then_inc(s["rden"], 1)
            dve.wait_ge(s["rden"], 1)
            dve.scalar_tensor_tensor(v(EM), pa[:, :, 1], 2.0, pd[:, :, 1], ALU.mult, ALU.mult).then_inc(s["em"], 1)
            dve.wait_ge(s["em"], 1)
            dve.scalar_tensor_tensor(pa[:], pa[:], 1.0, pd[:], ALU.add, ALU.mult).then_inc(s["pw"], 1)
            dve.wait_ge(s["cos"], 1)
            mul(v(RE), v(EM), ar[:, :, 1], s["f1"])
            mul(v(T1), v(T1), v(T1), s["f1"])
            dve.wait_ge(s["f1"], 2)
            dve.scalar_tensor_tensor(v(RE), v(T1), -2.0, v(RE), ALU.mult, ALU.add).then_inc(s["f1"], 1)
            dve.wait_ge(s["pw"], 1)
            mul(ar[:], ar[:], pa[:], s["ar"])
            mul(ai[:], ai[:], pa[:], s["ai"])
            dve.wait_ge(s["f1"], 3)
            mul(v(T1), par[:, 0, :], par[:, 0, :], s["f2"])
            mul(v(T2), par[:, 1, :], par[:, 1, :], s["f2"])
            dve.wait_ge(s["f2"], 2)
            mul(v(DEN), v(T1), v(T2), s["f2"], ALU.add)
            dve.wait_ge(s["f2"], 3)
            dve.reciprocal(v(DEN), v(DEN)).then_inc(s["den2"], 1)
            dve.wait_ge(s["ai"], 1)
            mul(v(T1), v(RE), par[:, 0, :], s["f3"])
            mul(v(T2), ai[:, :, 1], par[:, 1, :], s["f3"])
            mul(v(FI), ai[:, :, 1], par[:, 0, :], s["f3"])
            mul(v(T3), v(RE), par[:, 1, :], s["f3"])
            dve.wait_ge(s["f3"], 4)
            mul(v(T1), v(T1), v(T2), s["f4"], ALU.add)
            mul(v(FI), v(FI), v(T3), s["f4"], ALU.subtract)
            dve.wait_ge(s["f4"], 2)
            dve.wait_ge(s["den2"], 1)
            mul(v(FR), v(T1), v(DEN), s["f5"])
            mul(v(FI), v(FI), v(DEN), s["f5"])
            dve.wait_ge(s["f5"], 2)
            dve.wait_ge(s["in_b"], 32)
            mul(bx[:], b1[:], gm(v(FR)), s["bx1"])
            mul(by[:], b2[:], gm(v(FR)), s["by1"])
            mul(b2[:], b2[:], gm(v(FI)), s["bx1"])
            mul(b1[:], b1[:], gm(v(FI)), s["by1"])
            dve.wait_ge(s["bx1"], 2)
            dve.scalar_tensor_tensor(bx[:], b2[:], sgn, bx[:], ALU.mult, ALU.add).then_inc(s["bx"], 1)
            dve.wait_ge(s["by1"], 2)
            dve.scalar_tensor_tensor(by[:], by[:], sgn, b1[:], ALU.mult, ALU.subtract).then_inc(s["by"], 1)
            dve.wait_ge(s["in_c"], 32)
            dve.tensor_scalar(cx[:], c1i[:], nsgn, None, ALU.mult).then_inc(s["cx"], 1)
            dve.tensor_scalar(ncx[:], c1i[:], sgn, None, ALU.mult).then_inc(s["ncx"], 1)
            dve.tensor_scalar(nc2[:], c2i[:], -1.0, None, ALU.mult).then_inc(s["nc2"], 1)
            mul(sinc[:], gc(v(TU)), starts, s["cang"])
            dve.wait_ge(s["cang"], 1)
            dve.tensor_scalar(spm[:], sinc[:], ROUND, ROUND, ALU.add, ALU.subtract).then_inc(s["crnd"], 1)
            dve.wait_ge(s["crnd"], 1)
            mul(sinc[:], sinc[:], spm[:], s["cang"], ALU.subtract)
            dve.wait_ge(s["cang"], 2)
            dve.tensor_scalar(cosc[:], sinc[:], 0.25, None, ALU.add).then_inc(s["cang"], 1)
            dve.wait_ge(s["cang"], 3)
            dve.sem_inc(s["cfr"], 1)
            dve.tensor_scalar(spm[:], cosc[:], ROUND, ROUND, ALU.add, ALU.subtract).then_inc(s["crnd"], 1)
            dve.wait_ge(s["crnd"], 2)
            mul(cosc[:], cosc[:], spm[:], s["cang"], ALU.subtract)
            dve.wait_ge(s["cang"], 4)
            dve.sem_inc(s["cfr"], 1)
            dve.wait_ge(s["csin"], 1)
            dve.tensor_scalar(spm[:], sinc[:], nsgn, None, ALU.mult).then_inc(s["cspm"], 1)
            dve.wait_ge(s["ccos"], 1)
            dve.wait_ge(s["cspm"], 1)
            dve.wait_ge(s["bx"], 1)
            dve.wait_ge(s["by"], 1)
            dve.wait_ge(s["cx"], 1)
            dve.wait_ge(s["nc2"], 1)
            wide = lambda x, n: x.rearrange("p g (t a) -> p g t a", a=1).to_broadcast([P, OCT, n, M])
            over = lambda x, n: x.rearrange("p g (a n) -> p g a n", a=1).to_broadcast([P, OCT, n, M])

            def inputs(o):
                grp = bass.ds(o * OCT, OCT)
                dve.wait_ge(s["bt_ps"], o)
                mul(bp[:], wide(ar[:, grp, NK:NT], L), over(bx[:, grp, :], L), s["ba"])
                dve.wait_ge(s["c1"], o)
                mul(tmp[:, :, 0:L, :], wide(ai[:, grp, NK:NT], L), over(by[:, grp, :], L), s["ba"])
                dve.wait_ge(s["ba"], o * 2 + 2)
                mul(bp[:], bp[:], tmp[:, :, 0:L, :], s["bp"], ALU.add)

            def outputs(o, par, free=None):
                grp = bass.ds(o * OCT, OCT)
                dve.wait_ge(s["k_ps"], o)
                if free is not None:
                    dve.wait_ge(s["y_ps"], free)
                mul(c1[par][:], wide(ar[:, grp, 0:NK], NK), over(cx[:, grp, :], NK), s["c1a"])
                dve.tensor_copy(bxo[:], bx[:, grp, :]).then_inc(s["bxo"], 1)
                dve.wait_ge(s["bp"], o + 1)
                mul(tmp[:], wide(ai[:, grp, 0:NK], NK), over(nc2[:, grp, :], NK), s["c1a"])
                dve.wait_ge(s["c1a"], o * 2 + 2)
                mul(c1[par][:], c1[par][:], tmp[:], s["c1"], ALU.add)

            def step(o, par, last=False):
                grp = bass.ds(o * OCT, OCT)
                if not last:
                    inputs(o + 1)
                    outputs(o + 1, 1 - par, o)
                dve.wait_ge(s["v_ps"], o + 1)
                mul(z1[par], v_ps[:].rearrange("p (g c) -> p g c", g=OCT), cosc[:, grp, :], s["z1"])
                mul(z2[par], vs_ps[:].rearrange("p (g c) -> p g c", g=OCT), spm[:, grp, :], s["z1"])
                dve.wait_ge(s["z1"], o * 2 + 2)
                mul(z1[par], z1[par], z2[par], s["z2"], ALU.add)
                dve.wait_ge(s["z2"], o + 1)
                dve.wait_ge(s["w1"], o * 2)
                for g in range(OCT):
                    ins = dve.tensor_tensor_scan(
                        z[:, g, :], pa[:, bass.ds(o * OCT + g, 1), L].to_broadcast([P, NCH]), z1[par][:, g, :], 0.0,
                        ALU.mult, ALU.add)
                    ins.then_inc(s["scan"], 1)
                dve.wait_ge(s["scan"], o * OCT + OCT)
                mul(z1[par], z[:], cosc[:, grp, :], s["w1"])
                mul(z2[par], z[:], sinc[:, grp, :], s["w1"])

            inputs(0)
            outputs(0, 0)
            octets(dve, step)

        @block.tensor
        def _(pe):
            pe.wait_ge(s["in_ident"], 16)
            pe.wait_ge(s["in_u0"], 16 * L)
            pe.wait_ge(s["bx"], 1)

            def transpose_inputs(o):
                pe.wait_ge(s["bp"], o + 1)
                pe.wait_ge(s["bt"], o * 2)
                for g in range(OCT):
                    ins = pe.transpose(bt_ps[:, g * P:(g + 1) * P], bp[:, g, :, :].rearrange("p j m -> p (j m)"), ident[:])
                ins.then_inc(s["bt_ps"], 1)

            def responses(o, par):
                pe.wait_ge(s["c1"], o + 1)
                pe.wait_ge(s["bxo"], o + 1)
                pe.wait_ge(s["kpad"], o)
                for g in range(OCT):
                    ins = pe.matmul(k_ps[0:M, g * P:(g + 1) * P], bxo[:, g, :],
                                    c1[par][:, g, 0:L, :].rearrange("p t n -> p (t n)"), start=True, stop=True)
                ins.then_inc(s["k_ps"], 1)

            def chunk_sums(o):
                pe.wait_ge(s["bt"], o * 2 + 2)
                pe.wait_ge(s["z1"], o * 2)
                for g in range(OCT):
                    u_g = u_all[:, bass.ds(o * OCT + g, 1), :].rearrange("p a c -> p (a c)")
                    pe.matmul(v_ps[:, g * NCH:(g + 1) * NCH], bt[:, g, 0:P], u_g, start=True, stop=True)
                    ins = pe.matmul(vs_ps[:, g * NCH:(g + 1) * NCH], bt[:, g, ST:3 * ST], u_g, start=True, stop=True)
                ins.then_inc(s["v_ps"], 1)

            def step(o, par, last=False):
                if not last:
                    transpose_inputs(o + 1)
                    responses(o + 1, 1 - par)
                pe.wait_ge(s["w1"], o * 2 + 2)
                pe.wait_ge(s["c2"], o + 1)
                pe.wait_ge(s["t_in"], o * (16 * L) + 16 * L)
                pe.wait_ge(s["y_sb"], o)
                for g in range(OCT):
                    u_g = u_all[:, bass.ds(o * OCT + g, 1), :].rearrange("p a c -> p (a c)")
                    pe.matmul(y_ps[:, g * NCH:(g + 1) * NCH], t_sb[par][:, g, :], u_g, start=True, stop=False)
                    later = y_ps[:, g * NCH + 1:(g + 1) * NCH]
                    pe.matmul(later, c1[par][:, g, 1:NK, :].rearrange("p t n -> p (t n)"), z1[par][:, g, 0:NCH - 1],
                              start=False, stop=False)
                    ins = pe.matmul(later, c2[par][:, g, :, :].rearrange("p t n -> p (t n)"), z2[par][:, g, 0:NCH - 1],
                                    start=False, stop=True)
                ins.then_inc(s["y_ps"], 1)
                if not last:
                    chunk_sums(o + 1)

            transpose_inputs(0)
            responses(0, 0)
            chunk_sums(0)
            octets(pe, step)


def s5_output(nc, d, y_feat, sums):
    KS = KD // 2
    with ExitStack() as ctx:
        def sb(name, shape, dt=F32):
            return ctx.enter_context(nc.sbuf_tensor("l_" + name, shape, dt))

        s = sems(ctx, nc, "l", "sums_in u_in cols_in w0 w1 w2 yd gelu g_hi g_lo hi lo tile th half_b ya out0 out1")
        landed = (s["w0"], s["w1"], s["w2"])
        ya_out = (s["out0"], s["out1"])
        u_feat = sb("u", [P, KS, T])
        cols = sb("cols", [P, 3, KS])
        g = sb("g", [P, KS, T])
        g_hi, g_lo = sb("g_hi", [P, KS, T], F32R), sb("g_lo", [P, KS, T], F32R)
        w_raw = sb("w_raw", [P, RING, WCOLS])
        w_hi, w_lo = sb("w_hi", [P, 2, KS, 2 * P], F32R), sb("w_lo", [P, 2, KS, 2 * P], F32R)
        th = sb("th", [P, 2, T])
        banks = [ctx.enter_context(nc.psum_tensor(f"l_ps{i}", [P, T], F32)) for i in range(2)]
        block = ctx.enter_context(nc.Block())

        @block.sync
        def _(sp):
            sp.dma_start(u_feat[:], d["u"].rearrange("o p n -> p o n")).then_inc(s["u_in"], 16)
            sp.dma_start(cols[:, 0:2, :], d["s5_cols"]).then_inc(s["cols_in"], 16)
            for n in range(KS // 2):
                if n == RING:
                    sp.dma_start(sums[:], d["ada_sums"].rearrange("(a b) p n -> p a b n", b=2)).then_inc(s["sums_in"], 16)
                if n >= RING:
                    sp.wait_ge(s["lo"], n - RING + 1)
                sp.dma_start(w_raw[:, n % RING, :], d["w_glu"][n]).then_inc(landed[n % RING], 16)
            for j in range(KS):
                sp.wait_ge(s["ya"], j + 1)
                sp.dma_start(d["y_a"][j], th[:, j % 2, :]).then_inc(ya_out[j % 2], 16)
            sp.wait_ge(s["out0"], 16 * (KS // 2))
            sp.wait_ge(s["out1"], 16 * (KS // 2))
            sp.wait_ge(s["sums_in"], 16)

        @block.scalar
        def _(act):
            def tile(act, j):
                act.wait_ge(s["tile"], j + 1)
                act.wait_ge(s["half_b"], 1)
                if j >= 2:
                    act.wait_ge(ya_out[j % 2], 16 * (j // 2))
                act.activation(th[:, j % 2, :], banks[j % 2][:], ACT.Tanh, scale=0.5, bias=cols[:, 2, j:j + 1]
                               ).then_inc(s["th"], 1)

            for n in range(KS):
                act.wait_ge(s["yd"], n + 1)
                act.activation(g[:, n, :].rearrange("p (c i) -> p i c", i=8),
                               u_feat[:, n, :].rearrange("p (i c) -> p i c", i=8), ACT.Gelu_apprx_tanh).then_inc(s["gelu"], 1)
                act.wait_ge(s["gelu"], n + 1)
                act.activation(g_hi[:, n, :], g[:, n, :], ACT.Copy).then_inc(s["g_hi"], 1)
            for n in range(KS // 2):
                act.wait_ge(landed[n % RING], 16 * (n // RING + 1))
                if n >= 2:
                    act.wait_ge(s["tile"], 2 * n - 2)
                act.activation(w_hi[:, n % 2].rearrange("p k n -> p (k n)"), w_raw[:, n % RING, :], ACT.Copy
                               ).then_inc(s["hi"], 1)
                for j in range(2 * n - 2, 2 * n) if n else ():
                    tile(act, j)
            for j in range(KS - 2, KS):
                tile(act, j)

        @block.vector
        def _(dve):
            def out_tile(dve, j):
                dve.wait_ge(s["th"], j + 1)
                dve.scalar_tensor_tensor(th[:, j % 2, :], th[:, j % 2, :], 1.0, g[:, j, :], ALU.add, ALU.mult).then_inc(s["ya"], 1)

            dve.wait_ge(s["cols_in"], 16)
            dve.tensor_scalar(cols[:, 2, :], cols[:, 1, :], 0.5, None, ALU.mult).then_inc(s["half_b"], 1)
            dve.wait_ge(s["u_in"], 16)
            for n in range(KS):
                dve.scalar_tensor_tensor(u_feat[:, n, :], u_feat[:, n, :], cols[:, 0, n:n + 1], y_feat[:, n, :],
                                         ALU.mult, ALU.add).then_inc(s["yd"], 1)
            for n in range(KS):
                dve.wait_ge(s["g_hi"], n + 1)
                dve.tensor_tensor(g_lo[:, n, :], g[:, n, :], g_hi[:, n, :].bitcast(F32), ALU.subtract).then_inc(s["g_lo"], 1)
            for n in range(KS // 2):
                dve.wait_ge(s["hi"], n + 1)
                dve.tensor_tensor(w_lo[:, n % 2].rearrange("p k n -> p (k n)"), w_raw[:, n % RING, :],
                                  w_hi[:, n % 2].rearrange("p k n -> p (k n)").bitcast(F32), ALU.subtract).then_inc(s["lo"], 1)
                for j in range(2 * n - 2, 2 * n) if n else ():
                    out_tile(dve, j)
            for j in range(KS - 2, KS):
                out_tile(dve, j)

        @block.tensor
        def _(pe):
            pe.wait_ge(s["g_lo"], KS)
            for j in range(KS):
                n = j // 2
                pe.wait_ge(s["hi"], n + 1)
                pe.wait_ge(s["lo"], n + 1)
                if j >= 2:
                    pe.wait_ge(s["th"], j - 1)
                for k in range(KS):
                    one = slice(j % 2 * P, (j % 2 + 1) * P)
                    ins = split3(pe, banks[j % 2][:], w_hi[:, n % 2, k, one], w_lo[:, n % 2, k, one], g_hi[:, k, :],
                                 g_lo[:, k, :], k == 0, k == KS - 1)
                ins.then_inc(s["tile"], 1)


def modulation_rows(nc, d, sums):
    with ExitStack() as ctx:
        def sb(name, shape, dt=F32):
            return ctx.enter_context(nc.sbuf_tensor("m_" + name, shape, dt))

        s = sems(ctx, nc, "m", "bias_in ones_set sum sum_ps row out")
        bias = sb("bias", [1, 5, D])
        row = sb("row", [1, 4, D])
        ones = sb("ones", [P, 1])
        ps = ctx.enter_context(nc.psum_tensor("m_ps", [1, 2, D], F32))
        block = ctx.enter_context(nc.Block())

        @block.sync
        def _(sp):
            sp.dma_start(bias[:], d["mod_bias"]).then_inc(s["bias_in"], 16)
            sp.wait_ge(s["row"], 6)
            sp.dma_start(d["mod_rows"], row[:]).then_inc(s["out"], 16)
            sp.wait_ge(s["out"], 16)

        @block.vector
        def _(dve):
            dve.memset(ones[:], 1.0).then_inc(s["ones_set"], 1)
            for part in range(4):
                dve.tensor_tensor(sums[:, part, 0, :], sums[:, part, 0, :], sums[:, part, 1, :], ALU.add).then_inc(s["sum"], 1)
            dve.wait_ge(s["bias_in"], 16)
            for part in range(4):
                dve.wait_ge(s["sum_ps"], part + 1)
                dve.tensor_tensor(row[:, part, :], ps[:, part % 2, :], bias[:, part, :], ALU.add).then_inc(s["row"], 1)
            dve.wait_ge(s["row"], 4)
            dve.tensor_scalar(row[:, 0, :], row[:, 0, :], 0.5, None, ALU.mult).then_inc(s["row"], 1)
            dve.scalar_tensor_tensor(row[:, 2, :], row[:, 2, :], 1.0, bias[:, 4, :], ALU.add, ALU.mult).then_inc(s["row"], 1)

        @block.tensor
        def _(pe):
            pe.wait_ge(s["ones_set"], 1)
            for part in range(4):
                pe.wait_ge(s["sum"], part + 1)
                if part >= 2:
                    pe.wait_ge(s["row"], part - 1)
                for n in range(D // T):
                    ins = pe.matmul(ps[:, part % 2, n * T:(n + 1) * T], ones[:], sums[:, part, 0, n * T:(n + 1) * T],
                                    start=True, stop=True)
                ins.then_inc(s["sum_ps"], 1)


def merge(nc, d, m_hi, m_lo):
    KS = KD // 2
    with ExitStack() as ctx:
        def sb(name, shape, dt=F32):
            return ctx.enter_context(nc.sbuf_tensor("p_" + name, shape, dt))

        s = sems(ctx, nc, "p", "zeros blank0 blank1 w0 w1 w2 y_hi y_lo hi lo pa pb ma mb m m_hi m_lo",
                 d["program"], "y0 y1 y2 ga0 ga1 gb0 gb1")
        landed, y_in = (s["w0"], s["w1"], s["w2"]), (s["y0"], s["y1"], s["y2"])
        ga_in, gb_in = (s["ga0"], s["ga1"]), (s["gb0"], s["gb1"])
        y_raw = sb("y_raw", [P, RING, T])
        y_hi, y_lo = sb("y_hi", [P, KD, T], F32R), sb("y_lo", [P, KD, T], F32R)
        w_raw = sb("w_raw", [P, RING, WCOLS])
        w_hi, w_lo = sb("w_hi", [P, 2, KD, P], F32R), sb("w_lo", [P, 2, KD, P], F32R)
        ga, gb = sb("ga", [P, 2, T]), sb("gb", [P, 2, T])
        blank = (s["blank0"], s["blank1"])
        m = sb("m", [P, T])
        zeros = sb("zeros", [P, D // 2])
        banks = [[ctx.enter_context(nc.psum_tensor(f"p_ps{i}{j}", [P, T], F32)) for j in range(2)] for i in range(2)]
        block = ctx.enter_context(nc.Block())

        @block.sync
        def _(sp):
            for n in range(KD):
                if n >= RING:
                    sp.wait_ge(s["lo"], n - RING + 1)
                sp.dma_start(w_raw[:, n % RING, :], d["w_proj"][n]).then_inc(landed[n % RING], 16)

        @block.gpsimd
        def _(pool):
            for n in range(KD):
                if n >= RING:
                    pool.wait_ge(s["y_lo"], n - RING + 1)
                src = d["y_a"][n] if n < KS else d["y_b"][n - KS]
                pool.dma_start(y_raw[:, n % RING, :], src).then_inc(y_in[n % RING], 16)
            for n in range(KD):
                if n >= 2:
                    pool.wait_ge(s["m"], n - 1)
                tile = n // 2 * 4 + n % 2
                pool.dma_start(ga[:, n % 2, :], d["gates"][tile]).then_inc(ga_in[n % 2], 16)
                pool.dma_start(gb[:, n % 2, :], d["gates"][tile + 2]).then_inc(gb_in[n % 2], 16)

        @block.scalar
        def _(act):
            def hi(n):
                act.wait_ge(landed[n % RING], 16 * (n // RING + 1))
                if n >= 2:
                    act.wait_ge(s["pb"], n - 1)
                act.activation(w_hi[:, n % 2].rearrange("p k n -> p (k n)"), w_raw[:, n % RING, :], ACT.Copy
                               ).then_inc(s["hi"], 1)

            hi(0)
            act.wait_ge(s["zeros"], 1)
            for n in range(KD):
                act.wait_ge(y_in[n % RING], 16 * (n // RING + 1))
                act.activation(y_hi[:, n, :], y_raw[:, n % RING, :], ACT.Copy).then_inc(s["y_hi"], 1)
            for n in range(KD):
                if n + 1 < KD:
                    hi(n + 1)
                act.wait_ge(s["m"], n + 1)
                act.activation(m_hi[:, n, :], m[:], ACT.Copy).then_inc(s["m_hi"], 1)
                act.dma_start(d["y_moe"][ITEMS - KD + n].rearrange("p (a n) -> p a n", a=2),
                              zeros[:].unsqueeze(1).to_broadcast([P, 2, D // 2])).then_inc(blank[n % 2], 16)
                if n:
                    act.wait_ge(blank[(n - 1) % 2], 16 * ((n - 1) // 2 + 1))
            act.wait_ge(blank[(KD - 1) % 2], 16 * ((KD - 1) // 2 + 1))

        @block.vector
        def _(dve):
            def lo(n):
                dve.wait_ge(s["hi"], n + 1)
                dve.tensor_tensor(w_lo[:, n % 2].rearrange("p k n -> p (k n)"), w_raw[:, n % RING, :],
                                  w_hi[:, n % 2].rearrange("p k n -> p (k n)").bitcast(F32), ALU.subtract).then_inc(s["lo"], 1)

            dve.memset(zeros[:], 0.0).then_inc(s["zeros"], 1)
            lo(0)
            for n in range(KD):
                dve.wait_ge(s["y_hi"], n + 1)
                dve.tensor_tensor(y_lo[:, n, :], y_raw[:, n % RING, :], y_hi[:, n, :].bitcast(F32), ALU.subtract
                                  ).then_inc(s["y_lo"], 1)
            for n in range(KD):
                if n + 1 < KD:
                    lo(n + 1)
                a_ps, b_ps = banks[n % 2]
                dve.wait_ge(s["pa"], n + 1)
                dve.wait_ge(ga_in[n % 2], 16 * (n // 2 + 1))
                dve.scalar_tensor_tensor(ga[:, n % 2, :], ga[:, n % 2, :], 1.0, a_ps[:], ALU.add, ALU.mult).then_inc(s["ma"], 1)
                dve.wait_ge(s["pb"], n + 1)
                dve.wait_ge(gb_in[n % 2], 16 * (n // 2 + 1))
                dve.scalar_tensor_tensor(gb[:, n % 2, :], gb[:, n % 2, :], 1.0, b_ps[:], ALU.add, ALU.mult).then_inc(s["mb"], 1)
                dve.wait_ge(s["ma"], n + 1)
                dve.wait_ge(s["mb"], n + 1)
                if n:
                    dve.wait_ge(s["m_lo"], n)
                dve.scalar_tensor_tensor(m[:], ga[:, n % 2, :], 0.5, gb[:, n % 2, :], ALU.mult, ALU.add).then_inc(s["m"], 1)
                dve.wait_ge(s["m_hi"], n + 1)
                dve.tensor_tensor(m_lo[:, n, :], m[:], m_hi[:, n, :].bitcast(F32), ALU.subtract).then_inc(s["m_lo"], 1)

        @block.tensor
        def _(pe):
            for n in range(KD):
                pe.wait_ge(s["hi"], n + 1)
                pe.wait_ge(s["lo"], n + 1)
                for side in range(2):
                    if n >= 2:
                        pe.wait_ge((s["ma"], s["mb"])[side], n - 1)
                    for k in range(side * KS, (side + 1) * KS):
                        if n == 0:
                            pe.wait_ge(s["y_lo"], k + 1)
                        ins = split3(pe, banks[n % 2][side][:], w_hi[:, n % 2, k, :], w_lo[:, n % 2, k, :], y_hi[:, k, :],
                                     y_lo[:, k, :], k == side * KS, k == (side + 1) * KS - 1)
                    ins.then_inc((s["pa"], s["pb"])[side], 1)


def output_projection(nc, d, m_hi, m_lo, x2, ss, rows, router, ident):
    HALF = D // 2
    with ExitStack() as ctx:
        def sb(name, shape, dt=F32):
            return ctx.enter_context(nc.sbuf_tensor("o_" + name, shape, dt))

        s = sems(ctx, nc, "o", "w0 w1 w2 hi lo used mul x2 sq",
                 d["program"], "g_in x_in scale_in shift_in ident_in router_in")
        landed = (s["w0"], s["w1"], s["w2"])
        w_raw = sb("w_raw", [P, RING, WCOLS])
        w_hi, w_lo = sb("w_hi", [P, 2, 2, HALF], F32R), sb("w_lo", [P, 2, 2, HALF], F32R)
        g1 = sb("g1", [P, D])
        part = sb("part", [P, 2, T])
        sq = sb("sq", [P, D])
        banks = [ctx.enter_context(nc.psum_tensor(f"o_ps{i}", [P, T], F32)) for i in range(2 * NT)]
        block = ctx.enter_context(nc.Block())
        CHUNKS = KD

        @block.sync
        def _(sp):
            for n in range(CHUNKS):
                if n >= RING:
                    sp.wait_ge(s["lo"], n - RING + 1)
                sp.dma_start(w_raw[:, n % RING, :], d["w_out"][n]).then_inc(landed[n % RING], 16)

        @block.gpsimd
        def _(pool):
            pool.dma_start(g1[:], d["mod_rows"][0:1, 0, :].to_broadcast([P, D])).then_inc(s["g_in"], 16)
            pool.dma_start(x2[:], d["x"].rearrange("(t p) n -> p t n", p=P)).then_inc(s["x_in"], 16)
            pool.dma_start(rows[:, 0, :], d["mod_rows"][0:1, 2, :].to_broadcast([P, D])).then_inc(s["scale_in"], 16)
            pool.dma_start(rows[:, 1, :], d["mod_rows"][0:1, 1, :].to_broadcast([P, D])).then_inc(s["shift_in"], 16)
            pool.dma_start(ident[:], d["ident"]).then_inc(s["ident_in"], 16)
            pool.dma_start(router[:], d["w_router"]).then_inc(s["router_in"], 16)
            for loaded in ("scale_in", "shift_in", "ident_in", "router_in"):
                pool.wait_ge(s[loaded], 16)

        @block.scalar
        def _(act):
            for n in range(CHUNKS):
                act.wait_ge(landed[n % RING], 16 * (n // RING + 1))
                if n >= 2:
                    act.wait_ge(s["used"], n - 1)
                act.activation(w_hi[:, n % 2].rearrange("p k n -> p (k n)"), w_raw[:, n % RING, :], ACT.Copy
                               ).then_inc(s["hi"], 1)
            for t in range(NT):
                act.wait_ge(s["x2"], 2 * NT + 2 * t + 2)
                if t:
                    act.wait_ge(s["sq"], t)
                act.activation(sq[:], x2[:, t, :], ACT.Square, accum_out=ss[:, t:t + 1]).then_inc(s["sq"], 1)

        @block.vector
        def _(dve):
            def lo(n):
                dve.wait_ge(s["hi"], n + 1)
                dve.tensor_tensor(w_lo[:, n % 2].rearrange("p k n -> p (k n)"), w_raw[:, n % RING, :],
                                  w_hi[:, n % 2].rearrange("p k n -> p (k n)").bitcast(F32), ALU.subtract).then_inc(s["lo"], 1)

            def add(done):
                half, i = done // (2 * NT), done % (2 * NT)
                cols = slice(half * HALF + i % 2 * T, half * HALF + (i % 2 + 1) * T)
                dve.wait_ge(s["mul"], done + 1)
                dve.tensor_tensor(x2[:, i // 2, cols], x2[:, i // 2, cols], part[:, i % 2, :], ALU.add).then_inc(s["x2"], 1)

            lo(0)
            dve.wait_ge(s["g_in"], 16)
            dve.wait_ge(s["x_in"], 16)
            for half in range(2):
                for n in range(half * KD // 2, (half + 1) * KD // 2):
                    if n + 1 < CHUNKS:
                        lo(n + 1)
                dve.wait_ge(s["used"], (half + 1) * KD // 2)
                for i in range(2 * NT):
                    cols = slice(half * HALF + i % 2 * T, half * HALF + (i % 2 + 1) * T)
                    done = half * 2 * NT + i
                    if i >= 2 or half:
                        dve.wait_ge(s["x2"], done - 1)
                    dve.tensor_tensor(part[:, i % 2, :], banks[i][:], g1[:, cols], ALU.mult).then_inc(s["mul"], 1)
                    if done >= 1:
                        add(done - 1)
            add(4 * NT - 1)

        @block.tensor
        def _(pe):
            for n in range(CHUNKS):
                pe.wait_ge(s["hi"], n + 1)
                pe.wait_ge(s["lo"], n + 1)
                for t in range(NT):
                    tok = slice(t * P, (t + 1) * P)
                    if n == CHUNKS // 2:
                        pe.wait_ge(s["mul"], 2 * t + 2)
                    for kk in range(2):
                        k = n % (KD // 2) * 2 + kk
                        for c in range(2):
                            ins = split3(pe, banks[2 * t + c][:], m_hi[:, k, tok], m_lo[:, k, tok],
                                         w_hi[:, n % 2, kk, c * T:(c + 1) * T], w_lo[:, n % 2, kk, c * T:(c + 1) * T],
                                         k == 0, k == KD - 1)
                ins.then_inc(s["used"], 1)


def norm2_and_route(nc, d, x2, ss, rows, router, ident, pair_w, places, tokens, items):
    with ExitStack() as ctx:
        def sb(name, shape, dt=F32):
            return ctx.enter_context(nc.sbuf_tensor("r_" + name, shape, dt))

        s = sems(ctx, nc, "r", "set x2_out h2_out root rinv hs h2 tr ev_a ev_v logits scores "
                 "step pairs ranks zeroed",
                 d["program"], "row_in before_in ids_in filled sc0 sc1 sc2 sc3 sc4 sc5 sc6 sc7 tok_in")
        scattered = (s["sc0"], s["sc1"], s["sc2"], s["sc3"], s["sc4"], s["sc5"], s["sc6"], s["sc7"])
        scale, shift = rows[:, 0, :], rows[:, 1, :]
        h2 = sb("h2", [P, NT, D])
        h2t = sb("h2t", [P, KD, T])
        before = sb("before", [P, P])
        ones = sb("ones", [P, P])
        row = sb("row", [P, 2 * EXPERTS + GROUPS + ITEMS])
        ids = sb("ids", [P, NT], I32)
        eps = sb("eps", [P, 1])
        root, rinv = sb("root", [P, NT]), sb("rinv", [P, NT])
        none = sb("none", [P, EXPERTS])
        no_tokens = sb("no_tokens", [P, ITEMS], I32)
        scores, sel, sel2, pri = (sb(n, [P, NT, EXPERTS]) for n in ("scores", "sel", "sel2", "pri"))
        first, second, both = (sb(n, [P, NT, EXPERTS]) for n in ("first", "second", "both"))
        top, low = sb("top", [P, NT * GROUPS, 2]), sb("low", [P, NT * GROUPS, 2])
        g1, g2, g3 = (sb(n, [P, NT, GROUPS]) for n in ("g1", "g2", "g3"))
        m1, m2 = sb("m1", [P, NT]), sb("m2", [P, NT])
        s1, s2 = sb("s1", [P, NT]), sb("s2", [P, NT])
        tiles, ends, base = sb("tiles", [P, EXPERTS]), sb("ends", [P, EXPERTS]), sb("base", [P, EXPERTS])
        past = sb("past", [1, ITEMS, EXPERTS])
        item_f = sb("item_f", [1, ITEMS])
        tr_ps = [ctx.enter_context(nc.psum_tensor(f"r_tr{i}", [P, T], F32)) for i in range(4)]
        logit_ps = ctx.enter_context(nc.psum_tensor("r_logits", [P, T], F32))
        rank_ps = ctx.enter_context(nc.psum_tensor("r_ranks", [P, T], F32))
        block = ctx.enter_context(nc.Block())

        E = EXPERTS
        per_expert = lambda t: t[:, 0:NT * E].rearrange("p (t e) -> p t e", e=E)
        by_group = lambda t: t[:].rearrange("p t (g e) -> p (t g) e", g=GROUPS)
        order_e, order_g = row[:, 0:E], row[:, E:E + GROUPS]
        item_nr, bias = row[0:1, E + GROUPS:E + GROUPS + ITEMS], row[:, E + GROUPS + ITEMS:]

        def over_tiles(v, n):
            return v.unsqueeze(1).to_broadcast([P, NT, n])

        def over_last(v, n):
            return v[:].unsqueeze(2).to_broadcast([P, NT, n])

        @block.sync
        def _(sp):
            sp.wait_ge(s["h2"], NT)
            sp.dma_start(d["h2"].rearrange("(t p) n -> p t n", p=P), h2[:]).then_inc(s["h2_out"], 16)
            sp.dma_start(d["x2"].rearrange("(t p) n -> p t n", p=P), x2[:]).then_inc(s["x2_out"], 16)
            sp.wait_ge(s["x2_out"], 16)
            sp.wait_ge(s["h2_out"], 16)

        @block.gpsimd
        def _(pool):
            pool.memset(no_tokens[:], 0).then_inc(s["zeroed"], 1)
            pool.dma_start(row[:], d["route_rows"].to_broadcast([P, 2 * E + GROUPS + ITEMS])).then_inc(s["row_in"], 16)
            pool.dma_start(before[:], d["before"]).then_inc(s["before_in"], 16)
            pool.dma_start(ids[:], d["token_ids"]).then_inc(s["ids_in"], 16)
            pool.wait_ge(s["zeroed"], 1)
            pool.dma_start(d["tokens"].rearrange("(p i) o -> p (i o)", p=P), no_tokens[:]).then_inc(s["filled"], 16)
            pool.wait_ge(s["filled"], 16)
            pool.wait_ge(s["ids_in"], 16)
            pool.wait_ge(s["ranks"], 1)
            for n in range(2 * NT):
                pool.indirect_dma_start(d["tokens"], bass.IndirectOffsetOnAxis(ap=places[:, n:n + 1], axis=0),
                                        ids[:, n % NT:n % NT + 1], None).then_inc(scattered[n], 16)
            for n in range(2 * NT):
                pool.wait_ge(scattered[n], 16)
            pool.dma_start(tokens[:], d["tokens"].rearrange("(i p) o -> p (i o)", p=P), allow_slow_non_contiguous=True).then_inc(s["tok_in"], 16)
            pool.wait_ge(s["tok_in"], 16)

        @block.scalar
        def _(act):
            act.wait_ge(s["set"], 1)
            act.activation(root[:], ss[:], ACT.Sqrt, bias=eps[:, 0:1], scale=1.0 / D).then_inc(s["root"], 1)
            for n in range(0, 4 * NT, 2):
                act.wait_ge(s["tr"], n + 1)
                act.activation(h2t[:, n % 4 * 4:n % 4 * 4 + 4, n // 4 * P:(n // 4 + 1) * P],
                               tr_ps[n % 4][:].rearrange("p (k n) -> p k n", k=4), ACT.Copy).then_inc(s["ev_a"], 1)
            act.wait_ge(s["logits"], 1)
            act.activation(scores[:], per_expert(logit_ps), ACT.Sigmoid).then_inc(s["scores"], 1)

        @block.vector
        def _(dve):
            count = 0

            def done(ins):
                nonlocal count
                count += 1
                ins.then_inc(s["step"], 1)
                dve.wait_ge(s["step"], count)

            dve.memset(eps[:], EPS).then_inc(s["set"], 1)
            dve.memset(none[:], 0.0).then_inc(s["set"], 1)
            dve.memset(ones[:], 1.0).then_inc(s["set"], 1)
            dve.wait_ge(s["root"], 1)
            dve.reciprocal(rinv[:], root[:]).then_inc(s["rinv"], 1)
            dve.wait_ge(s["rinv"], 1)

            def evacuate(t):
                for n in (4 * t + 1, 4 * t + 3):
                    dve.wait_ge(s["tr"], n + 1)
                    dve.tensor_copy(h2t[:, n % 4 * 4:n % 4 * 4 + 4, t * P:(t + 1) * P],
                                    tr_ps[n % 4][:].rearrange("p (k n) -> p k n", k=4)).then_inc(s["ev_v"], 1)

            for t in range(NT):
                dve.scalar_tensor_tensor(h2[:, t, :], x2[:, t, :], rinv[:, t:t + 1], scale, ALU.mult, ALU.mult
                                         ).then_inc(s["hs"], 1)
                dve.wait_ge(s["hs"], t + 1)
                dve.tensor_tensor(h2[:, t, :], h2[:, t, :], shift, ALU.add).then_inc(s["h2"], 1)
                if t:
                    evacuate(t - 1)
            evacuate(NT - 1)

            dve.wait_ge(s["scores"], 1)
            dve.wait_ge(s["row_in"], 16)
            done(dve.tensor_tensor(sel[:], scores[:], over_tiles(bias, E), ALU.add))
            x = sel[:].rearrange("p t (g a b) -> p (t g) a b", g=GROUPS, a=2)
            done(dve.tensor_tensor(top[:], x[:, :, :, 0], x[:, :, :, 1], ALU.max))
            done(dve.tensor_tensor(low[:], x[:, :, :, 0], x[:, :, :, 1], ALU.min))
            flat = lambda t: t[:].rearrange("p t g -> p (t g)")
            done(dve.tensor_tensor(flat(g1), top[:, :, 0], top[:, :, 1], ALU.max))
            done(dve.tensor_tensor(flat(g2), top[:, :, 0], top[:, :, 1], ALU.min))
            done(dve.tensor_tensor(flat(g3), low[:, :, 0], low[:, :, 1], ALU.max))
            done(dve.tensor_tensor(g2[:], g2[:], g3[:], ALU.max))
            done(dve.tensor_tensor(g1[:], g1[:], g2[:], ALU.add))

            def one_hot(out, values, order, n, work):
                done(dve.tensor_reduce(m1[:], values[:], AX.X, ALU.max))
                done(dve.tensor_tensor(work[:], values[:], over_last(m1, n), ALU.is_equal))
                done(dve.tensor_tensor(work[:], work[:], over_tiles(order, n), ALU.mult))
                done(dve.tensor_reduce(m2[:], work[:], AX.X, ALU.max))
                done(dve.tensor_tensor(out[:], work[:], over_last(m2, n), ALU.is_equal))

            one_hot(g3, g1, order_g, GROUPS, g2)
            done(dve.tensor_scalar(g1[:], g3[:], 1.0, -NEG, ALU.subtract, ALU.mult))
            in_group = lambda g: flat(g).unsqueeze(2).to_broadcast([P, NT * GROUPS, E // GROUPS])
            done(dve.tensor_tensor(by_group(sel2), by_group(sel), in_group(g3), ALU.mult))
            done(dve.tensor_tensor(by_group(sel2), by_group(sel2), in_group(g1), ALU.add))
            one_hot(first, sel2, order_e, E, pri)
            done(dve.scalar_tensor_tensor(sel2[:], first[:], 2 * NEG, sel2[:], ALU.mult, ALU.add))
            one_hot(second, sel2, order_e, E, pri)
            done(dve.tensor_tensor(both[:], first[:], second[:], ALU.add))
            dve.sem_inc(s["pairs"], 1)

            for total, hot in ((s1, first), (s2, second)):
                done(dve.tensor_tensor(pri[:], scores[:], hot[:], ALU.mult))
                done(dve.tensor_reduce(total[:], pri[:], AX.X, ALU.add))
            done(dve.tensor_tensor(m1[:], s1[:], s2[:], ALU.add))
            done(dve.reciprocal(m2[:], m1[:]))
            for n, total in enumerate((s1, s2)):
                done(dve.scalar_tensor_tensor(pair_w[:, n * NT:(n + 1) * NT], total[:], 0.5, m2[:], ALU.mult, ALU.mult))

            dve.wait_ge(s["logits"], 2)
            counts = rank_ps[:, NT * E:(NT + 1) * E]
            done(dve.tensor_scalar(tiles[:], counts, 0.0, None, ALU.is_gt))
            for n in range(1, NT):
                done(dve.scalar_tensor_tensor(tiles[:], counts, float(n * P), tiles[:], ALU.is_gt, ALU.add))
            done(dve.tensor_tensor_scan(ends[:], tiles[:], none[:], 0.0, ALU.add, ALU.add))
            done(dve.tensor_tensor(base[:], ends[:], tiles[:], ALU.subtract))
            done(dve.tensor_scalar(base[:], base[:], float(P), None, ALU.mult))
            done(dve.tensor_tensor(sel[:], per_expert(rank_ps), over_tiles(base[:], E), ALU.add))
            for n, hot in enumerate((first, second)):
                done(dve.tensor_tensor(pri[:], sel[:], hot[:], ALU.mult))
                done(dve.tensor_reduce(m1[:], pri[:], AX.X, ALU.add))
                done(dve.tensor_copy(places[:, n * NT:(n + 1) * NT], m1[:]))
            dve.sem_inc(s["ranks"], 1)
            ends0 = ends[0:1, :].unsqueeze(1).to_broadcast([1, ITEMS, E])
            done(dve.tensor_tensor(past[:], item_nr.unsqueeze(2).to_broadcast([1, ITEMS, E]), ends0, ALU.is_ge))
            done(dve.tensor_reduce(item_f[:], past[:], AX.X, ALU.add))
            done(dve.tensor_scalar(item_f[:], item_f[:], float(E - 1), None, ALU.min))
            done(dve.tensor_copy(items[0:1, 1:1 + ITEMS], item_f[:]))
            done(dve.tensor_copy(items[0:1, 0:1], ends[0:1, E - 1:E]))

        @block.tensor
        def _(pe):
            def logits(t):
                pe.wait_ge(s["ev_a"], 2 * t + 2)
                pe.wait_ge(s["ev_v"], 2 * t + 2)
                for k in range(KD):
                    ins = pe.matmul(logit_ps[:, t * E:(t + 1) * E], h2t[:, k, t * P:(t + 1) * P], router[:, k, :],
                                    start=(k == 0), stop=(k == KD - 1))
                return ins

            for t in range(NT):
                pe.wait_ge(s["h2"], t + 1)
                for n in range(4 * t, 4 * t + 4):
                    if t:
                        pe.wait_ge(s["ev_v"] if n % 2 else s["ev_a"], n // 2 - 1)
                    for kk in range(4):
                        k = n % 4 * 4 + kk
                        ins = pe.transpose(tr_ps[n % 4][:, kk * P:(kk + 1) * P], h2[:, t, k * P:(k + 1) * P], ident[:])
                    ins.then_inc(s["tr"], 1)
                if t:
                    logits(t - 1)
            logits(NT - 1).then_inc(s["logits"], 1)
            pe.wait_ge(s["pairs"], 1)
            pe.wait_ge(s["before_in"], 16)
            pe.wait_ge(s["set"], 3)
            for t in range(NT + 1):
                out = rank_ps[:, t * E:(t + 1) * E]
                if t < NT:
                    pe.matmul(out, before[:], both[:, t, :], start=True, stop=(t == 0))
                for u in range(t):
                    ins = pe.matmul(out, ones[:], both[:, u, :], start=(t == NT and u == 0), stop=(u == t - 1))
            ins.then_inc(s["logits"], 1)


def experts(nc, d, tokens, items, x2, gate, norm):
    RAW, SPLIT = 4, 3
    HF = D // 4
    with ExitStack() as ctx:
        def sb(name, shape, dt=F32):
            return ctx.enter_context(nc.sbuf_tensor("e_" + name, shape, dt))

        s = sems(ctx, nc, "e", "w0 w1 w2 w3 idx idx_seen hi lo used xt x_hi x_lo th sg hid hid_t ht_hi ht_lo y_a y_v "
                 "y_out end gate_in norm_in x_in",
                 d["program"], "ident_in xg")
        landed = (s["w0"], s["w1"], s["w2"], s["w3"])
        w_raw = sb("w_raw", [P, RAW, WCOLS])
        w_hi, w_lo = sb("w_hi", [P, SPLIT, WCOLS], F32R), sb("w_lo", [P, SPLIT, WCOLS], F32R)
        x_rows = sb("x_rows", [P, D])
        x_hi, x_lo = sb("x_hi", [P, KD, P], F32R), sb("x_lo", [P, KD, P], F32R)
        silu = sb("silu", [P, HF])
        hid = sb("hid", [P, 2, HF])
        hid_hi, hid_lo = sb("hid_hi", [P, 8, P], F32R), sb("hid_lo", [P, 8, P], F32R)
        y = sb("y", [P, D])
        ident = sb("ident", [P, P])
        idx = sb("idx", [P, 1], U32)
        banks = [ctx.enter_context(nc.psum_tensor(f"e_ps{i}", [P, T], F32)) for i in range(8)]
        block = ctx.enter_context(nc.Block())

        def count(eng):
            return eng.value_load(items[0:1, 0:1], min_val=8, max_val=ITEMS - 1)

        def hi(act, c, landings, used):
            act.wait_ge(landed[c % RAW], landings)
            if used is not None:
                act.wait_ge(s["used"], used)
            act.activation(w_hi[:, c % SPLIT, :], w_raw[:, c % RAW, :], ACT.Copy).then_inc(s["hi"], 1)

        def lo(dve, c, hi_done):
            dve.wait_ge(s["hi"], hi_done)
            dve.tensor_tensor(w_lo[:, c % SPLIT, :], w_raw[:, c % RAW, :], w_hi[:, c % SPLIT, :].bitcast(F32),
                              ALU.subtract).then_inc(s["lo"], 1)

        def x_bank(g):
            return banks[1 + 2 * (g % 2)]

        def x_part(t, g):
            return t[:, 4 * g:4 * g + 4, :].rearrange("p k n -> p (k n)")

        @block.sync
        def _(sp):
            first = sp.value_load(items[0:1, 1:2], min_val=0, max_val=EXPERTS - 1)
            sp.dma_start(w_raw[:, 0, :], d["w_experts"][bass.ds(first * ECH, 1)].rearrange("a p n -> (a p) n")
                         ).then_inc(landed[0], 16)
            sp.dma_start(gate[:], d["mod_rows"][0:1, 3, :].to_broadcast([P, D])).then_inc(s["gate_in"], 16)
            sp.dma_start(norm[:], d["final_norm_w"].to_broadcast([P, D])).then_inc(s["norm_in"], 16)
            sp.dma_start(x2[:], d["x2"].rearrange("(t p) n -> p t n", p=P)).then_inc(s["x_in"], 16)
            n_items = count(sp)
            with sp.Fori(0, n_items) as i:
                here = sp.value_load(items[0:1, bass.ds(i + 1, 1)], min_val=0, max_val=EXPERTS - 1)
                for c in range(1, ECH):
                    sp.wait_ge(s["lo"], i * ECH + (c + 1))
                    sp.dma_start(w_raw[:, c % RAW, :], d["w_experts"][bass.ds(here * ECH + c, 1)
                                 ].rearrange("a p n -> (a p) n")).then_inc(landed[c % RAW], 16)
                after = sp.value_load(items[0:1, bass.ds(i + 2, 1)], min_val=0, max_val=EXPERTS - 1)
                sp.wait_ge(s["lo"], i * ECH + (ECH + 1))
                sp.dma_start(w_raw[:, 0, :], d["w_experts"][bass.ds(after * ECH, 1)].rearrange("a p n -> (a p) n")
                             ).then_inc(landed[0], 16)
            for loaded in (s["gate_in"], s["norm_in"], s["x_in"]):
                sp.wait_ge(loaded, 16)

        @block.gpsimd
        def _(pool):
            pool.dma_start(ident[:], d["ident"]).then_inc(s["ident_in"], 16)
            pool.tensor_copy(idx[:], tokens[:, 0:1]).then_inc(s["idx"], 1)
            pool.wait_ge(s["idx"], 1)
            pool.indirect_dma_start(x_rows[:], None, d["h2"], bass.IndirectOffsetOnAxis(ap=idx[:], axis=0)
                                    ).then_inc(s["xg"], 16)
            n_items = count(pool)
            with pool.Fori(0, n_items) as i:
                pool.wait_ge(s["xg"], i * 16 + 16)
                pool.tensor_copy(idx[:], tokens[:, bass.ds(i + 1, 1)]).then_inc(s["idx"], 1)
                pool.wait_ge(s["xt"], i * 4 + 4)
                pool.sem_inc(s["idx_seen"], 1)
                pool.wait_ge(s["idx"], i + 2)
                pool.sem_inc(s["idx_seen"], 1)
                pool.wait_ge(s["ident_in"], 16)
                pool.indirect_dma_start(x_rows[:], None, d["h2"], bass.IndirectOffsetOnAxis(ap=idx[:], axis=0)
                                        ).then_inc(s["xg"], 16)

        @block.scalar
        def _(act):
            def x_group(g, before):
                act.wait_ge(s["xt"], before + g + 1)
                act.activation(x_part(x_hi, g), x_bank(g)[:], ACT.Copy).then_inc(s["x_hi"], 1)

            hi(act, 0, 16, None)
            for g in range(4):
                x_group(g, 0)
            n_items = count(act)
            with act.Fori(0, n_items) as i:
                for c in range(ECH):
                    nxt = c + 1
                    hi(act, nxt % ECH, i * (16 * ECH // RAW) + 16 * (nxt // RAW + 1), i * ECH + (nxt + 1))
                    if c in (4, 12):
                        half = c // 12
                        act.wait_ge(s["used"], i * ECH + (c + SPLIT))
                        act.wait_ge(s["hid"], i * 2 + half)
                        act.activation(silu[:], banks[2 * half][:], ACT.Tanh, scale=0.5).then_inc(s["th"], 1)
                    if c in (11, 19):
                        half = c // 19
                        act.wait_ge(s["hid_t"], i * 2 + (half + 1))
                        act.activation(x_part(hid_hi, half), banks[2 * half][:], ACT.Copy).then_inc(s["ht_hi"], 1)
                    if c >= 20:
                        x_group(c - 20, i * 4 + 4)
                act.wait_ge(s["used"], i * ECH + (ECH + SPLIT))
                act.wait_ge(s["y_out"], i * 16)
                for n in range(2):
                    act.activation(y[:, n * T:(n + 1) * T], banks[4 + n][:], ACT.Copy).then_inc(s["y_a"], 1)
                act.wait_ge(s["y_a"], i * 2 + 2)
                act.wait_ge(s["y_v"], i * 2 + 2)
                act.dma_start(d["y_moe"][bass.ds(i, 1)].rearrange("a p n -> (a p) n"), y[:]).then_inc(s["y_out"], 16)
            act.wait_ge(s["y_out"], n_items * 16)
            act.sem_inc(s["end"], 1)

        @block.vector
        def _(dve):
            def x_group(g, before):
                dve.wait_ge(s["x_hi"], before + g + 1)
                dve.tensor_tensor(x_part(x_lo, g), x_bank(g)[:], x_part(x_hi, g).bitcast(F32), ALU.subtract
                                  ).then_inc(s["x_lo"], 1)

            dve.sem_inc(s["lo"], RAW)
            lo(dve, 0, 1)
            for g in range(4):
                x_group(g, 0)
            n_items = count(dve)
            with dve.Fori(0, n_items) as i:
                for c in range(ECH):
                    nxt = c + 1
                    lo(dve, nxt % ECH, i * ECH + (nxt + 1))
                    if c in (5, 13):
                        half = c // 13
                        dve.wait_ge(s["th"], i * 2 + (half + 1))
                        dve.scalar_tensor_tensor(silu[:], silu[:], 1.0, banks[2 * half][:], ALU.add, ALU.mult
                                                 ).then_inc(s["sg"], 1)
                    if c in (8, 16):
                        half = c // 16
                        dve.wait_ge(s["used"], i * ECH + (c + SPLIT))
                        dve.wait_ge(s["sg"], i * 2 + (half + 1))
                        dve.tensor_tensor(hid[:, half, :], silu[:], banks[2 * half + 1][:], ALU.mult).then_inc(s["hid"], 1)
                    if c in (12, 19):
                        half = c // 19
                        dve.wait_ge(s["ht_hi"], i * 2 + (half + 1))
                        dve.tensor_tensor(x_part(hid_lo, half), banks[2 * half][:], x_part(hid_hi, half).bitcast(F32),
                                          ALU.subtract).then_inc(s["ht_lo"], 1)
                    if c >= 20:
                        x_group(c - 20, i * 4 + 4)
                dve.wait_ge(s["used"], i * ECH + (ECH + SPLIT))
                dve.wait_ge(s["y_out"], i * 16)
                for n in range(2, 4):
                    dve.tensor_copy(y[:, n * T:(n + 1) * T], banks[4 + n][:]).then_inc(s["y_v"], 1)

        @block.tensor
        def _(pe):
            def x_group(g, before):
                if g >= 2:
                    pe.wait_ge(s["x_lo"], before + g - 1)
                for kk in range(4):
                    k = 4 * g + kk
                    ins = pe.transpose(x_bank(g)[:, kk * P:(kk + 1) * P], x_rows[:, k * P:(k + 1) * P], ident[:])
                ins.then_inc(s["xt"], 1)

            pe.sem_inc(s["used"], SPLIT)
            pe.wait_ge(s["ident_in"], 16)
            pe.wait_ge(s["xg"], 16)
            for g in range(4):
                x_group(g, 0)
            n_items = count(pe)
            with pe.Fori(0, n_items) as i:
                for c in range(ECH):
                    if c == 0:
                        pe.wait_ge(s["x_lo"], i * 4 + 4)
                    if c in (16, 20):
                        pe.wait_ge(s["ht_lo"], i * 2 + (c - 12) // 4)
                    if c == 16:
                        pe.wait_ge(s["y_a"], i * 2)
                        pe.wait_ge(s["y_v"], i * 2)
                    pe.wait_ge(s["lo"], i * ECH + (c + 1 + RAW))
                    if c < 16:
                        for kk in range(4):
                            k = c % 4 * 4 + kk
                            w = slice(kk * T, (kk + 1) * T)
                            ins = split3(pe, banks[c // 4][:], x_hi[:, k, :], x_lo[:, k, :], w_hi[:, c % SPLIT, w],
                                         w_lo[:, c % SPLIT, w], k == 0, k == KD - 1)
                    else:
                        k = c - 16
                        for n in range(4):
                            w = slice(n * T, (n + 1) * T)
                            ins = split3(pe, banks[4 + n][:], hid_hi[:, k, :], hid_lo[:, k, :], w_hi[:, c % SPLIT, w],
                                         w_lo[:, c % SPLIT, w], k == 0, k == 7)
                    ins.then_inc(s["used"], 1)
                    if c in (9, 17):
                        half = c // 17
                        pe.wait_ge(s["hid"], i * 2 + (half + 1))
                        for kk in range(4):
                            ins = pe.transpose(banks[2 * half][:, kk * P:(kk + 1) * P], hid[:, half, kk * P:(kk + 1) * P],
                                               ident[:])
                        ins.then_inc(s["hid_t"], 1)
                    if 18 <= c < 22:
                        if c == 18:
                            pe.wait_ge(s["xg"], i * 16 + 32)
                        x_group(c - 18, i * 4 + 4)


def combine_and_final_norm(nc, d, pair_w, places, x2, gate, norm):
    with ExitStack() as ctx:
        def sb(name, shape, dt=F32):
            return ctx.enter_context(nc.sbuf_tensor("f_" + name, shape, dt))

        s = sems(ctx, nc, "f", "eps wa wab gm x3 ss root rinv out o0 o1 o2 o3",
                 d["program"], "a0 a1 a2 a3 b0 b1 b2 b3")
        a_in, b_in = (s["a0"], s["a1"], s["a2"], s["a3"]), (s["b0"], s["b1"], s["b2"], s["b3"])
        stored = (s["o0"], s["o1"], s["o2"], s["o3"])
        ya, yb = sb("ya", [P, NT, D]), sb("yb", [P, NT, D])
        sq = sb("sq", [P, D])
        eps = sb("eps", [P, 1])
        ss, root, rinv = sb("ss", [P, NT]), sb("root", [P, NT]), sb("rinv", [P, NT])
        block = ctx.enter_context(nc.Block())

        @block.sync
        def _(sp):
            for t in range(NT):
                sp.wait_ge(s["out"], t + 1)
                sp.dma_start(d["out"][t * P:(t + 1) * P, :], ya[:, t, :]).then_inc(stored[t], 16)
            for t in range(NT):
                sp.wait_ge(stored[t], 16)

        @block.gpsimd
        def _(pool):
            rows = d["y_moe"].rearrange("i p n -> (i p) n")
            for t in range(NT):
                for n, (y, landed) in enumerate(((ya, a_in), (yb, b_in))):
                    c = n * NT + t
                    pool.indirect_dma_start(y[:, t, :], None, rows,
                                            bass.IndirectOffsetOnAxis(ap=places[:, c:c + 1], axis=0)
                                            ).then_inc(landed[t], 16)
            for t in range(NT):
                pool.wait_ge(s["wab"], t + 1)
                pool.tensor_tensor(yb[:, t, :], yb[:, t, :], gate[:], ALU.mult).then_inc(s["gm"], 1)

        @block.scalar
        def _(act):
            act.wait_ge(s["eps"], 1)
            def weighted(t):
                act.wait_ge(a_in[t], 16)
                act.activation(ya[:, t, :], ya[:, t, :], ACT.Copy, scale=pair_w[:, t:t + 1]).then_inc(s["wa"], 1)

            for t in range(NT):
                if t == 0:
                    weighted(0)
                if t + 1 < NT:
                    weighted(t + 1)
                act.wait_ge(s["x3"], t + 1)
                act.activation(sq[:], yb[:, t, :], ACT.Square, accum_out=ss[:, t:t + 1]).then_inc(s["ss"], 1)
                act.wait_ge(s["ss"], t + 1)
                act.activation(root[:, t:t + 1], ss[:, t:t + 1], ACT.Sqrt, bias=eps[:, 0:1], scale=1.0 / D
                               ).then_inc(s["root"], 1)

        @block.vector
        def _(dve):
            dve.memset(eps[:], EPS).then_inc(s["eps"], 1)

            def out(t):
                dve.wait_ge(s["root"], t + 1)
                dve.reciprocal(rinv[:, t:t + 1], root[:, t:t + 1]).then_inc(s["rinv"], 1)
                dve.wait_ge(s["rinv"], t + 1)
                dve.scalar_tensor_tensor(ya[:, t, :], yb[:, t, :], rinv[:, t:t + 1], norm[:], ALU.mult, ALU.mult
                                         ).then_inc(s["out"], 1)

            def weighted(t):
                dve.wait_ge(s["wa"], t + 1)
                dve.wait_ge(b_in[t], 16)
                dve.scalar_tensor_tensor(yb[:, t, :], yb[:, t, :], pair_w[:, NT + t:NT + t + 1], ya[:, t, :], ALU.mult,
                                         ALU.add).then_inc(s["wab"], 1)

            weighted(0)
            for t in range(NT):
                if t + 1 < NT:
                    weighted(t + 1)
                dve.wait_ge(s["gm"], t + 1)
                dve.tensor_tensor(yb[:, t, :], yb[:, t, :], x2[:, t, :], ALU.add).then_inc(s["x3"], 1)
                if t:
                    out(t - 1)
            out(NT - 1)


def build(nc, d, program):
    def scratch(name, shape, dt=F32):
        d[name] = nc.dram_tensor(name, shape, dt).ap()

    scratch("c_act", (P, KD))
    scratch("u", (HEADS, P, T))
    scratch("gates", (4 * HEADS, P, T))
    scratch("y_a", (HEADS, P, T))
    scratch("y_b", (HEADS, P, T))
    scratch("ada_sums", (HEADS, P, D))
    scratch("mod_rows", (1, 4, D))
    scratch("s5_k", (8, 16, 8, 240))
    scratch("s5_y", (HEADS, P, T))
    scratch("x2", (T, D))
    scratch("h2", (T, D))
    scratch("tokens", (ITEMS * P, 1), I32)
    scratch("y_moe", (ITEMS, P, D))
    d["program"] = program
    with ExitStack() as ctx:
        h_hi = ctx.enter_context(nc.sbuf_tensor("h_hi", [P, KD, T], F32R))
        h_lo = ctx.enter_context(nc.sbuf_tensor("h_lo", [P, KD, T], F32R))
        adaln_and_first_norm(nc, d, h_hi, h_lo)
        projections_and_gdn(nc, d, h_hi, h_lo)
    with ExitStack() as ctx:
        y_feat = ctx.enter_context(nc.sbuf_tensor("y_feat", [P, KD // 2, T], F32))
        s5_branch(nc, d, y_feat)
        sums = ctx.enter_context(nc.sbuf_tensor("mod_sums", [P, 4, 2, D], F32))
        s5_output(nc, d, y_feat, sums)
        modulation_rows(nc, d, sums)
    with ExitStack() as ctx:
        pair_w = ctx.enter_context(nc.sbuf_tensor("pair_w", [P, 2 * NT], F32))
        places = ctx.enter_context(nc.sbuf_tensor("places", [P, 2 * NT], U32))
        tokens = ctx.enter_context(nc.sbuf_tensor("token_at", [P, ITEMS], I32))
        items = ctx.enter_context(nc.sbuf_tensor("items", [1, 1 + ITEMS + 1], I32))
        with ExitStack() as inner:
            m_hi = inner.enter_context(nc.sbuf_tensor("m_hi", [P, KD, T], F32R))
            m_lo = inner.enter_context(nc.sbuf_tensor("m_lo", [P, KD, T], F32R))
            merge(nc, d, m_hi, m_lo)
            x2 = inner.enter_context(nc.sbuf_tensor("x2_sb", [P, NT, D], F32))
            ss = inner.enter_context(nc.sbuf_tensor("x2_ss", [P, NT], F32))
            rows = inner.enter_context(nc.sbuf_tensor("norm2_rows", [P, 2, D], F32))
            router = inner.enter_context(nc.sbuf_tensor("router", [P, KD, EXPERTS], F32))
            ident = inner.enter_context(nc.sbuf_tensor("ident", [P, P], F32))
            output_projection(nc, d, m_hi, m_lo, x2, ss, rows, router, ident)
            norm2_and_route(nc, d, x2, ss, rows, router, ident, pair_w, places, tokens, items)
        gate = ctx.enter_context(nc.sbuf_tensor("gate2", [P, D], F32))
        norm = ctx.enter_context(nc.sbuf_tensor("final_norm", [P, D], F32))
        x2 = ctx.enter_context(nc.sbuf_tensor("x2_again", [P, NT, D], F32))
        experts(nc, d, tokens, items, x2, gate, norm)
        combine_and_final_norm(nc, d, pair_w, places, x2, gate, norm)


def lay_out(x, c, w_ada, b_ada, norm1_w, norm2_w, w_in, s5_a_re, s5_a_im, s5_log_dt, s5_b_re, s5_b_im, s5_c_re,
            s5_c_im, s5_d, s5_w_glu, s5_b_glu, gdn_conv_w, gdn_a_log, gdn_dt_bias, gdn_norm_w, w_proj_a, w_proj_b,
            w_out, w_router, router_bias, w_gate, w_up, w_down, final_norm_w):
    cols = lambda v: v.reshape(-1, P).T
    arrays = {}
    arrays["c"] = cols(c[0])
    arrays["xT"] = x[0].T.reshape(KD, P, T).transpose(1, 0, 2)
    arrays["w_ada"] = w_ada[0]
    parts = b_ada[0].reshape(6, D)
    arrays["ada_cols"] = np.stack([cols(parts[0]), cols(parts[1]), cols(norm1_w[0])], axis=1)
    arrays["w_mod"] = w_ada[0].reshape(KD, P, 6, D)[:, :, 2:, :].transpose(2, 0, 1, 3).reshape(4 * KD, P, D)

    w = w_in[0]
    S = D // 2
    u, q, k, v, z = (w[:, i * S:(i + 1) * S] for i in range(5))
    b, a = w[:, 5 * S:5 * S + HEADS], w[:, 5 * S + HEADS:5 * S + 2 * HEADS]
    gates = w[:, 5 * S + 2 * HEADS:]
    first = np.zeros((D, P), np.float32)
    first[:, 0:8] = b
    first[:, 32:40] = a
    tiles = [first]
    for h in range(HEADS):
        one = slice(h * P, (h + 1) * P)
        tiles += [k[:, one], q[:, one], v[:, one], z[:, one], u[:, one]]
        for g in range(2):
            tiles += [gates[:, g * D + (2 * h + i) * P:g * D + (2 * h + i + 1) * P] for i in range(2)]
    tiles += [np.zeros((D, P), np.float32)] * 2
    arrays["w_in"] = np.stack(tiles).reshape(-1, KD, P, P).transpose(0, 2, 1, 3).reshape(-1, P, WCOLS)
    conv = gdn_conv_w[0].reshape(4, 3, HEADS, P)[:, [1, 0, 2]]
    arrays["conv_w"] = conv.transpose(3, 2, 1, 0).reshape(P, HEADS * 12)
    arrays["gdn_norm_w"] = gdn_norm_w[0][:, None]
    arrays["gdn_cols"] = np.stack([gdn_dt_bias[0], gdn_a_log[0]], axis=1)

    both = lambda v: np.concatenate([v, v], axis=0)
    arrays["s5_par"] = np.stack([both(s5_a_re[0].T), both(s5_a_im[0].T), np.broadcast_to(s5_log_dt[0], (P, 64))], axis=1)
    halves = lambda re, im: np.stack([np.concatenate([re, im], axis=0), np.concatenate([im, re], axis=0)], axis=1)
    arrays["s5_b"] = halves(s5_b_re[0].transpose(1, 0, 2), s5_b_im[0].transpose(1, 0, 2))
    arrays["s5_c"] = halves(s5_c_re[0].transpose(2, 0, 1), s5_c_im[0].transpose(2, 0, 1))
    arrays["s5_cols"] = np.stack([cols(s5_d[0]), cols(s5_b_glu[0])], axis=1)
    arrays["w_glu"] = s5_w_glu[0].reshape(KD // 2, P, KD // 4, 2 * P).transpose(2, 1, 0, 3).reshape(KD // 4, P, WCOLS)

    arrays["mod_bias"] = np.stack([parts[2], parts[3], parts[4], parts[5], norm2_w[0]])[None]
    tile_cols = lambda w: w.reshape(KD // 2, P, KD, P).transpose(2, 1, 0, 3)
    arrays["w_proj"] = np.concatenate([tile_cols(w_proj_a[0]), tile_cols(w_proj_b[0])], axis=2).reshape(KD, P, WCOLS)
    arrays["w_out"] = w_out[0].reshape(KD // 2, 2, P, 2, D // 2).transpose(3, 0, 2, 1, 4).reshape(KD, P, WCOLS)
    arrays["x"] = x[0]
    arrays["final_norm_w"] = final_norm_w[None, :]
    arrays["w_router"] = w_router.reshape(KD, P, EXPERTS).transpose(1, 0, 2)
    halves_ = lambda w: w[0].reshape(EXPERTS, 4, 4, P, 2, T).transpose(0, 4, 1, 3, 2, 5).reshape(EXPERTS, 2, 1, 4, P, WCOLS)
    up_down = np.concatenate([halves_(w_gate), halves_(w_up)], axis=2).reshape(EXPERTS, 16, P, WCOLS)
    arrays["w_experts"] = np.concatenate([up_down, w_down[0].reshape(EXPERTS, 8, P, D)], axis=1).reshape(-1, P, D)

    e_ = np.arange(EXPERTS)
    route = np.concatenate([EXPERTS - e_, GROUPS - np.arange(GROUPS), np.arange(ITEMS), router_bias])
    arrays["route_rows"] = route[None, :].astype(np.float32)
    arrays["before"] = (np.arange(P)[:, None] < np.arange(P)[None, :]).astype(np.float32)
    arrays["token_ids"] = np.arange(T).reshape(T // P, P).T.astype(np.int32)
    sign = np.where(np.arange(P)[:, None] < P // 2, -1.0, 1.0)
    row = np.concatenate([np.arange(9), np.arange(7, -1, -1), 8 * np.arange(64)])[None, :]
    arrays["s5_const"] = np.concatenate([np.broadcast_to(row, (P, 81)), sign, -sign], axis=1).astype(np.float32)
    arrays["ident"] = np.eye(P, dtype=np.float32)
    s_, c_ = np.arange(P)[:, None], np.arange(P)[None, :]
    arrays["causal"] = np.where(s_ <= c_, 0.0, NEG).astype(np.float32)
    level = lambda n: (s_ // 2**n == c_ // 2**n) & (s_ % 2**n < 2**(n - 1)) & (c_ % 2**n >= 2**(n - 1))
    arrays["masks"] = np.stack([level(n) for n in range(1, LEVELS + 1)], axis=1).astype(np.float32)
    return {n: np.ascontiguousarray(v) for n, v in arrays.items()}


def kernel(**inputs):
    import numpy as _np
    import concourse.bacc as _bacc
    from concourse import mybir as _mybir
    from concourse.bass_utils import run_bass_kernel_spmd as _run

    nc = _bacc.Bacc("TRN2", target_bir_lowering=False, num_devices=1)
    laid_out = lay_out(**{n: _np.asarray(v) for n, v in inputs.items()})
    arrays, tensors = {}, {}
    for name, a in laid_out.items():
        arrays[f"in_{name}_dram"] = a
        tensors[name] = nc.dram_tensor(f"in_{name}_dram", a.shape, _mybir.dt.from_np(a.dtype), kind="ExternalInput").ap()
    tensors["out"] = nc.dram_tensor("out_0_dram", (T, D), _mybir.dt.float32, kind="ExternalOutput").ap()
    with ExitStack() as program:
        build(nc, tensors, program)
    r = _run(nc, [arrays], core_ids=[0])
    return r.results[0]["out_0_dram"].reshape(1, T, D)
```
